# Optimizing a Trainium2 kernel written in Bass

```python
import math
import jax, jax.numpy as jnp
from jax import lax
import numpy as np

D_MODEL = 2048
BATCH = 1
SEQ = 256
DEPTH = 2

HEAD_DIM = 128
EPS = 1e-6
NEG = -1e30

NUM_BUCKETS = 32
MAX_DISTANCE = 2048

NSA_HEADS = 8
NSA_GROUPS = 2
NSA_HPG = NSA_HEADS // NSA_GROUPS
NSA_BLOCK = 64
NSA_TOPK = 16
NSA_WINDOW = 512
NSA_QCHUNK = 32

DIL_PAIRS = ((128, 1), (512, 4), (2048, 16))
DIL_GROUPS = 3
DIL_HPG = 4
DIL_HEADS = DIL_GROUPS * DIL_HPG
DIL_QCHUNK = 32

MLA_HEADS = 16
MLA_Q_RANK = 1536
MLA_KV_RANK = 512
MLA_NOPE = 128
MLA_ROPE = 64
MLA_V = 128
MLA_QBLOCK = 128
ROPE_THETA = 10000.0

A_Q = NSA_HEADS * HEAD_DIM
A_KV = 6 * NSA_GROUPS * HEAD_DIM
A_G3 = 3 * NSA_HEADS
A_GATE = NSA_HEADS * HEAD_DIM
B_QKV = 3 * DIL_HEADS * HEAD_DIM
B_GATE = DIL_HPG * HEAD_DIM
EVEN_IN = A_Q + A_KV + A_G3 + A_GATE + B_QKV + B_GATE
EVEN_MIX = A_GATE + B_GATE
ODD_MIX = MLA_HEADS * MLA_V
ODD_IN = MLA_Q_RANK + MLA_KV_RANK + MLA_ROPE + ODD_MIX

kernel_name = "hybrid_nsa_dilated_mla_trunk"

def _split_points(widths):
    pts, acc = [], 0
    for w in widths[:-1]:
        acc += w
        pts.append(acc)
    return pts

def rmsnorm(x, w):
    xf = x.astype(jnp.float32)
    y = xf * lax.rsqrt(jnp.mean(xf * xf, axis=-1, keepdims=True) + EPS)
    return (y * w.astype(jnp.float32)).astype(x.dtype)

def t5_bucket(dist):
    max_exact = NUM_BUCKETS // 2
    d = jnp.maximum(dist, 0)
    df = jnp.maximum(d, 1).astype(jnp.float32)
    large = max_exact + (jnp.log(df / max_exact) / math.log(MAX_DISTANCE / max_exact)
                         * (NUM_BUCKETS - max_exact)).astype(jnp.int32)
    large = jnp.minimum(large, NUM_BUCKETS - 1)
    return jnp.where(d < max_exact, d, large)

def masked_softmax(s, mask):
    p = jax.nn.softmax(jnp.where(mask, s, NEG), axis=-1)
    return jnp.where(mask, p, 0.0)

def rope(x, pos):
    half = x.shape[-1] // 2
    freqs = 1.0 / (ROPE_THETA ** (jnp.arange(half, dtype=jnp.float32) / half))
    ang = pos.astype(jnp.float32)[:, None] * freqs[None, :]
    cos = jnp.cos(ang)[:, None, :]
    sin = jnp.sin(ang)[:, None, :]
    xf = x.astype(jnp.float32)
    x1, x2 = xf[..., :half], xf[..., half:]
    return jnp.concatenate([x1 * cos - x2 * sin, x1 * sin + x2 * cos], axis=-1).astype(x.dtype)

def nsa_compress(kv, pos, w1, w2):
    b_, t_ = kv.shape[:2]
    nblk = t_ // NSA_BLOCK
    blk = kv.reshape(b_, nblk, NSA_BLOCK, NSA_GROUPS, HEAD_DIM) + pos[None, None, :, None, :]
    blk = blk.transpose(0, 1, 3, 2, 4).reshape(b_, nblk, NSA_GROUPS, NSA_BLOCK * HEAD_DIM)
    return jax.nn.silu(blk @ w1) @ w2

def nsa_attention(q, kv_all, gate_logits, cmp_pos, cmp_w1, cmp_w2, table):
    b_, t_ = q.shape[:2]
    L, W, QC, G, HPG = NSA_BLOCK, NSA_WINDOW, NSA_QCHUNK, NSA_GROUPS, NSA_HPG
    nblk = t_ // L
    nsel = min(NSA_TOPK, nblk)
    kc, vc, ks, vs, kw, vw = [a.reshape(b_, t_, G, HEAD_DIM) for a in jnp.split(kv_all, 6, axis=-1)]
    k_cmp = nsa_compress(kc, cmp_pos[0], cmp_w1[0], cmp_w2[0])
    v_cmp = nsa_compress(vc, cmp_pos[1], cmp_w1[1], cmp_w2[1])
    ks_blk = ks.reshape(b_, nblk, L, G, HEAD_DIM).transpose(0, 3, 1, 2, 4)
    vs_blk = vs.reshape(b_, nblk, L, G, HEAD_DIM).transpose(0, 3, 1, 2, 4)
    kw_pad = jnp.pad(kw, ((0, 0), (W, 0), (0, 0), (0, 0)))
    vw_pad = jnp.pad(vw, ((0, 0), (W, 0), (0, 0), (0, 0)))
    tab = table[:, :NSA_HEADS].reshape(NUM_BUCKETS, G, HPG)
    cmp_end = jnp.arange(nblk) * L + (L - 1)
    blk_ids = jnp.arange(nblk)
    scale = HEAD_DIM ** -0.5
    nc = t_ // QC
    q_chunks = q.reshape(b_, nc, QC, G, HPG, HEAD_DIM).transpose(1, 0, 2, 3, 4, 5)
    bidx = jnp.arange(b_)[:, None, None, None]
    gidx = jnp.arange(G)[None, :, None, None]

    def chunk(args):
        qb, c = args
        t = c * QC + jnp.arange(QC)
        s = jnp.einsum('bqghd,bngd->bghqn', qb, k_cmp).astype(jnp.float32) * scale
        dist = t[:, None] - cmp_end[None, :]
        s = s + tab[t5_bucket(dist)].transpose(2, 3, 0, 1)[None]
        p_cmp = masked_softmax(s, dist >= 0)
        o_cmp = jnp.einsum('bghqn,bngd->bqghd', p_cmp.astype(v_cmp.dtype), v_cmp)
        imp = p_cmp.sum(axis=2)
        cur = t // L
        forced = (blk_ids[None, :] == 0) | (blk_ids[None, :] == cur[:, None]) | (blk_ids[None, :] == cur[:, None] - 1)
        imp = jnp.where(forced, jnp.inf, jnp.where(blk_ids[None, :] > cur[:, None], -jnp.inf, imp))
        _, sel = lax.top_k(imp, nsel)
        k_sel = ks_blk[bidx, gidx, sel]
        v_sel = vs_blk[bidx, gidx, sel]
        s = jnp.einsum('bqghd,bgqskd->bghqsk', qb, k_sel).astype(jnp.float32) * scale
        kpos = sel[..., None] * L + jnp.arange(L)
        dist = t[None, None, :, None, None] - kpos
        bias = tab[t5_bucket(dist), jnp.arange(G)[None, :, None, None, None]]
        s = (s + bias.transpose(0, 1, 5, 2, 3, 4)).reshape(b_, G, HPG, QC, nsel * L)
        mask = (dist >= 0)[:, :, None].reshape(b_, G, 1, QC, nsel * L)
        p = masked_softmax(s, mask).reshape(b_, G, HPG, QC, nsel, L)
        o_slc = jnp.einsum('bghqsk,bgqskd->bqghd', p.astype(v_sel.dtype), v_sel)
        kwin = lax.dynamic_slice_in_dim(kw_pad, c * QC, W + QC, axis=1)
        vwin = lax.dynamic_slice_in_dim(vw_pad, c * QC, W + QC, axis=1)
        kp = c * QC - W + jnp.arange(W + QC)
        dist = t[:, None] - kp[None, :]
        mask = (dist >= 0) & (dist < W) & (kp[None, :] >= 0)
        s = jnp.einsum('bqghd,bkgd->bghqk', qb, kwin).astype(jnp.float32) * scale
        s = s + tab[t5_bucket(dist)].transpose(2, 3, 0, 1)[None]
        p = masked_softmax(s, mask)
        o_win = jnp.einsum('bghqk,bkgd->bqghd', p.astype(vwin.dtype), vwin)
        return o_cmp, o_slc, o_win

    o_cmp, o_slc, o_win = lax.map(chunk, (q_chunks, jnp.arange(nc)))

    def unchunk(a):
        return a.transpose(1, 0, 2, 3, 4, 5).reshape(b_, t_, NSA_HEADS, HEAD_DIM)

    g = jax.nn.sigmoid(gate_logits.astype(jnp.float32)).reshape(b_, t_, NSA_HEADS, 3, 1).astype(q.dtype)
    out = g[:, :, :, 0] * unchunk(o_cmp) + g[:, :, :, 1] * unchunk(o_slc) + g[:, :, :, 2] * unchunk(o_win)
    return out.reshape(b_, t_, NSA_HEADS * HEAD_DIM)

def dilated_attention(q, k, v, table):
    b_, t_ = q.shape[:2]
    QC = DIL_QCHUNK
    nc = t_ // QC
    scale = HEAD_DIM ** -0.5
    tab = table[:, NSA_HEADS:].reshape(NUM_BUCKETS, DIL_GROUPS, DIL_HPG)
    k_groups = [k[:, :, g] for g in range(DIL_GROUPS)]
    v_groups = [v[:, :, g] for g in range(DIL_GROUPS)]
    biases = []
    for g, (w, d) in enumerate(DIL_PAIRS):
        offs = jnp.arange(w // d + 1) * d
        biases.append(tab[t5_bucket(offs), g])
    q_chunks = q.reshape(b_, nc, QC, DIL_GROUPS, DIL_HPG, HEAD_DIM).transpose(1, 0, 2, 3, 4, 5)

    def chunk(args):
        qb, c = args
        t = c * QC + jnp.arange(QC)
        outs, lses = [], []
        for g, (w, d) in enumerate(DIL_PAIRS):
            m = w // d + 1
            idx = t[:, None] - jnp.arange(m)[None, :] * d
            valid = idx >= 0
            idxc = jnp.maximum(idx, 0)
            kg = k_groups[g][:, idxc]
            vg = v_groups[g][:, idxc]
            s = jnp.einsum('bqhd,bqmhd->bhqm', qb[:, :, g], kg).astype(jnp.float32) * scale
            s = jnp.where(valid[None, None], s + biases[g].T[None, :, None, :], NEG)
            lse = jax.nn.logsumexp(s, axis=-1)
            p = jnp.exp(s - lse[..., None])
            outs.append(jnp.einsum('bhqm,bqmhd->bqhd', p.astype(vg.dtype), vg))
            lses.append(lse)
        alpha = jax.nn.softmax(jnp.stack(lses, 0), axis=0)
        o = jnp.einsum('gbhq,gbqhd->bqhd', alpha, jnp.stack(outs, 0).astype(jnp.float32))
        return o.astype(q.dtype)

    o = lax.map(chunk, (q_chunks, jnp.arange(nc)))
    return o.transpose(1, 0, 2, 3, 4).reshape(b_, t_, DIL_HPG * HEAD_DIM)

def mla_attention(cq, ckv, kpe, q_norm, w_qb, kv_norm, w_kvb):
    b_, t_ = cq.shape[:2]
    H, QB = MLA_HEADS, MLA_QBLOCK
    pos = jnp.arange(t_)
    q = (rmsnorm(cq, q_norm) @ w_qb).reshape(b_, t_, H, MLA_NOPE + MLA_ROPE)
    q_nope, q_pe = q[..., :MLA_NOPE], rope(q[..., MLA_NOPE:], pos)
    kv = (rmsnorm(ckv, kv_norm) @ w_kvb).reshape(b_, t_, H, MLA_NOPE + MLA_V)
    k_nope, v = kv[..., :MLA_NOPE], kv[..., MLA_NOPE:]
    k_pe = rope(kpe[:, :, None, :], pos)[:, :, 0]
    scale = (MLA_NOPE + MLA_ROPE) ** -0.5
    nb = t_ // QB
    qn = q_nope.reshape(b_, nb, QB, H, MLA_NOPE).transpose(1, 0, 2, 3, 4)
    qp = q_pe.reshape(b_, nb, QB, H, MLA_ROPE).transpose(1, 0, 2, 3, 4)

    def block(args):
        qnb, qpb, c = args
        t = c * QB + jnp.arange(QB)
        s = (jnp.einsum('bqhd,bkhd->bhqk', qnb, k_nope)
             + jnp.einsum('bqhd,bkd->bhqk', qpb, k_pe)).astype(jnp.float32) * scale
        p = masked_softmax(s, pos[None, :] <= t[:, None])
        return jnp.einsum('bhqk,bkhd->bqhd', p.astype(v.dtype), v)

    o = lax.map(block, (qn, qp, jnp.arange(nb)))
    return o.transpose(1, 0, 2, 3, 4).reshape(b_, t_, H * MLA_V)

def setup_inputs(seed: int = 0) -> dict:
    key = jax.random.key(seed)
    ks = jax.random.split(key, 16)
    ne = (DEPTH + 1) // 2
    no = DEPTH // 2

    def nrm(k, shape, scale):
        return jax.random.normal(k, shape, jnp.float32) * scale

    return {
        "x": nrm(ks[0], (BATCH, SEQ, D_MODEL), 1.0),
        "rel_bias": nrm(ks[1], (NUM_BUCKETS, NSA_HEADS + DIL_HEADS), 0.2),
        "norm_w": 1.0 + nrm(ks[2], (DEPTH, D_MODEL), 0.02),
        "final_norm_w": 1.0 + nrm(ks[3], (D_MODEL,), 0.02),
        "ev_w_in": nrm(ks[4], (ne, D_MODEL, EVEN_IN), D_MODEL ** -0.5),
        "nsa_cmp_pos": nrm(ks[5], (ne, 2, NSA_BLOCK, HEAD_DIM), 0.1),
        "nsa_cmp_w1": nrm(ks[6], (ne, 2, NSA_BLOCK * HEAD_DIM, HEAD_DIM), (NSA_BLOCK * HEAD_DIM) ** -0.5),
        "nsa_cmp_w2": nrm(ks[7], (ne, 2, HEAD_DIM, HEAD_DIM), HEAD_DIM ** -0.5),
        "ev_w_out": nrm(ks[8], (ne, EVEN_MIX, D_MODEL), 0.5 * EVEN_MIX ** -0.5),
        "od_w_in": nrm(ks[9], (no, D_MODEL, ODD_IN), D_MODEL ** -0.5),
        "mla_q_norm": 1.0 + nrm(ks[10], (no, MLA_Q_RANK), 0.02),
        "mla_w_qb": nrm(ks[11], (no, MLA_Q_RANK, MLA_HEADS * (MLA_NOPE + MLA_ROPE)), MLA_Q_RANK ** -0.5),
        "mla_kv_norm": 1.0 + nrm(ks[12], (no, MLA_KV_RANK), 0.02),
        "mla_w_kvb": nrm(ks[13], (no, MLA_KV_RANK, MLA_HEADS * (MLA_NOPE + MLA_V)), MLA_KV_RANK ** -0.5),
        "od_w_out": nrm(ks[14], (no, ODD_MIX, D_MODEL), 0.5 * ODD_MIX ** -0.5),
    }

def reference(x, rel_bias, norm_w, final_norm_w, ev_w_in, nsa_cmp_pos, nsa_cmp_w1, nsa_cmp_w2,
              ev_w_out, od_w_in, mla_q_norm, mla_w_qb, mla_kv_norm, mla_w_kvb, od_w_out):
    b_, t_ = x.shape[:2]
    even_pts = _split_points([A_Q, A_KV, A_G3, A_GATE, B_QKV, B_GATE])
    odd_pts = _split_points([MLA_Q_RANK, MLA_KV_RANK, MLA_ROPE, ODD_MIX])
    for l in range(DEPTH):
        h = rmsnorm(x, norm_w[l])
        i = l // 2
        if l % 2 == 0:
            z = h @ ev_w_in[i]
            q_a, kv_a, g3_a, gate_a, qkv_b, gate_b = jnp.split(z, even_pts, axis=-1)
            o_a = nsa_attention(q_a.reshape(b_, t_, NSA_HEADS, HEAD_DIM), kv_a, g3_a,
                                nsa_cmp_pos[i], nsa_cmp_w1[i], nsa_cmp_w2[i], rel_bias)
            q_b, k_b, v_b = [a.reshape(b_, t_, DIL_GROUPS, DIL_HPG, HEAD_DIM)
                             for a in jnp.split(qkv_b, 3, axis=-1)]
            o_b = dilated_attention(q_b, k_b, v_b, rel_bias)
            mixed = jnp.concatenate([o_a * jax.nn.silu(gate_a), o_b * jax.nn.silu(gate_b)], axis=-1)
            x = x + mixed @ ev_w_out[i]
        else:
            z = h @ od_w_in[i]
            cq, ckv, kpe, gate_c = jnp.split(z, odd_pts, axis=-1)
            o_c = mla_attention(cq, ckv, kpe, mla_q_norm[i], mla_w_qb[i], mla_kv_norm[i], mla_w_kvb[i])
            x = x + (o_c * jax.nn.silu(gate_c)) @ od_w_out[i]
    return rmsnorm(x, final_norm_w)


_drawn_inputs = setup_inputs


def setup_inputs(seed=0):
    import zlib

    import numpy as np

    out = dict(_drawn_inputs(seed))
    spreads = {}
    factors = {'rel_bias': 5.492,
     'norm_w': 8.0,
     'final_norm_w': 2.941,
     'nsa_cmp_pos': 7.598,
     'mla_q_norm': 8.0,
     'mla_kv_norm': 8.0}
    for name, (base, spread) in spreads.items():
        noise = np.random.default_rng([zlib.crc32(name.encode()), seed]).standard_normal(out[name].shape)
        drawn = base * np.exp(spread * noise) if base else spread * noise
        out[name] = __import__('jax').numpy.asarray(drawn.astype(out[name].dtype))
    for name, factor in factors.items():
        out[name] = (out[name] * factor).astype(out[name].dtype)
    return out
```

```python
import math
from contextlib import ExitStack

import numpy as np
import concourse.bass as bass
from concourse import mybir

P = 128
D_MODEL, SEQ, HD = 2048, 256, 128
EPS, NEG = 1e-6, -1e30
NT = SEQ // P
KD = D_MODEL // P
BUCKETS, MAX_DIST = 32, 2048
NSA_HEADS, NSA_GROUPS, NSA_BLOCK = 8, 2, 64
NSA_HPG = NSA_HEADS // NSA_GROUPS
NCMP = SEQ // NSA_BLOCK
DIL = ((128, 1), (512, 4), (2048, 16))
DG, DH = 3, 4
HEADS_B = NSA_HEADS + DG * DH
MH, QR, KVR, NOPE, ROPE, MV = 16, 1536, 512, 128, 64, 128
KQ, KKV = QR // P, KVR // P
EVEN_MIX = NSA_HEADS + DH
PB = 8
PW = PB * P
R = 4
XR = 4
LEAD = R - 1
TW = 3 * P
RRW = 3 * P

N_V, N_DIL = 0, NT * 2 * PB
N_KSW = N_DIL + DH * 16
N_NSA = N_KSW + 8
N_WOE = N_NSA + NSA_HEADS * 4
N_LAT = N_WOE + KD * EVEN_MIX // PB
N_PE = N_LAT + 2 * (KQ + KKV + 1)
N_VM = N_PE + (MH // 2) * KQ // PB
N_MLA = N_VM + 8
N_WOO = N_MLA + MH * 4
N_END = N_WOO + 2 * KD
T_DIL = 8
T_KSW = T_DIL + DH * 8
T_NSA = T_KSW + 4
T_WOE = T_NSA + NSA_HEADS * 2
T_LAT = T_WOE + KD
T_PE = T_LAT + KQ + KKV + 1
T_VM = T_PE + MH // 2
T_MLA = T_VM + 8
T_WOO = T_MLA + MH * 3
MID_WOE, MID_PE = 0, 9
MID_MLA = MID_PE + MH // 4
MID_WOO = MID_MLA + MH
A_NSA = DH
A_MLA = A_NSA + NSA_HEADS
G_NSA = DH * DG
G_MLA = G_NSA + NSA_HEADS * 3
U_BIAS, U_CBIAS, U_NORM0, U_GATE3, U_CMP, U_CMP2, U_NORM1, U_NORMQ, U_NORMKV, U_NORMF = range(10)
DVE_TURN = {"dil": 4, "nsa": 6, "lat": 4, "mla": 6, "woo": 8}


class Tally:

    def __init__(self, eng, sem):
        self.eng, self.sem, self.base, self.n = eng, sem, 0, 0

    def link(self, ins):
        ins.then_inc(self.sem, 1)
        self.n += 1
        self.eng.wait_ge(self.sem, self.base + self.n)

    def turn(self, i, per_turn):
        self.entry, self.per = self.base + self.n, per_turn
        self.base, self.n = self.entry + i * per_turn, 0

    def leave(self, turns):
        assert self.n == self.per, (self.n, self.per)
        self.base, self.n = self.entry + turns * self.per, 0


def trunk(nc, x_in, w_stream, w_gate3, w_cmp1, w_cmp2, cmp_pos, table, norms, q_norm, kv_norm,
          onehot, onehot_cmp, row_mask, cmp_mask, cmp_valid, causal, rope_cs, ident_in, y_out):
    f32, f32r = mybir.dt.float32, mybir.dt.float32r
    ALU, ACT, AX = mybir.AluOpType, mybir.ActivationFunctionType, mybir.AxisListType
    MUL, ADD, SUB, MAX = ALU.mult, ALU.add, ALU.subtract, ALU.max
    ROOT = math.sqrt(HD)
    SC_EVEN, SC_MLA = HD ** -0.5, (NOPE + ROPE) ** -0.5
    ds = bass.ds

    x_mid = nc.dram_tensor("x_mid", (P, KD, SEQ), f32)
    bias_rows = nc.dram_tensor("bias_rows", (HEADS_B, P, RRW), f32)

    ctx = ExitStack()
    with ctx:
        def sb(name, shape, dt=f32, into=ctx):
            return into.enter_context(nc.sbuf_tensor(name, shape, dt))

        def sem(name):
            return ctx.enter_context(nc.semaphore(name))

        hH, hL = sb("hH", [P, KD, SEQ], f32r), sb("hL", [P, KD, SEQ], f32r)
        raw = sb("raw", [P, R, PW])
        wH, wL = sb("wH", [P, R, PW], f32r), sb("wL", [P, R, PW], f32r)
        vt = sb("vt", [P, NT, D_MODEL])
        xr = sb("xr", [P, XR, SEQ])
        rfac = sb("rfac", [P, SEQ + NT])
        rq = sb("rq", [P, SEQ + NT])
        rkv = sb("rkv", [P, SEQ + NT])
        rtmp, rvar = sb("rtmp", [P, SEQ + NT]), sb("rvar", [P, SEQ + NT])
        gate_z, gate_t, gate_g = sb("gate_z", [P, SEQ]), sb("gate_t", [P, SEQ]), sb("gate_g", [P, SEQ])
        mixf = sb("mixf", [P, SEQ])
        mx, nmx = sb("mx", [P, NT, DG]), sb("nmx", [P, NT, DG])
        den, coef = sb("den", [P, NT, DG]), sb("coef", [P, NT, DG])
        mx1, tick = sb("mx1", [P, NT]), sb("tick", [P, 16])
        ident, ones = sb("ident", [P, P]), sb("ones", [P, P])
        nrm = sb("nrm", [P, 3, KD])
        qn, kvn = sb("qn", [P, KQ]), sb("kvn", [P, KKV])
        zt, zw = sb("zt", [P, 2, SEQ]), sb("zw", [P, 2, SEQ])
        zs = sb("zs", [P, SEQ])
        rnew = sb("rnew", [P, SEQ + NT])
        sq, acc = sb("sq", [P, 2, SEQ]), sb("acc", [P, SEQ])
        nrm_sum = sb("nrm_sum", [P, SEQ])

        start = ExitStack()
        xT = sb("xT", [P, KD, SEQ], into=start)
        sq0 = sb("sq0", [P, 2, 4, SEQ], into=start)
        oneh = sb("oneh", [BUCKETS, RRW], into=start)
        oneh_c = sb("oneh_c", [BUCKETS, NT * NCMP, P], into=start)
        start.close()
        mixH, mixL = sb("mixH", [P, KD, SEQ], f32r), sb("mixL", [P, KD, SEQ], f32r)

        even = ExitStack()
        qd, kd = sb("qd", [P, DG, SEQ], into=even), sb("kd", [P, DG, SEQ], into=even)
        probs_e = sb("probs_e", [P, DG, TW], into=even)
        probsT_e = sb("probsT_e", [P, DG, TW], into=even)
        v_cur = sb("v_cur", [P, DG, NT, P], into=even)
        kvc = sb("kvc", [P, 4, SEQ], into=even)
        ksw = sb("ksw", [P, 4, SEQ], into=even)
        qa = sb("qa", [P, SEQ], into=even)
        kcp = sb("kcp", [P, 2, NSA_BLOCK, NSA_GROUPS * NCMP], into=even)
        w1 = sb("w1", [P, 2, PW], into=even)
        w2 = sb("w2", [P, 2, P], into=even)
        posT = sb("posT", [P, 2, NSA_BLOCK], into=even)
        cz, ct, cs = [sb(n, [P, 2, 8], into=even) for n in ("cz", "ct", "cs")]
        kcmp = sb("kcmp", [P, 8], into=even)
        vcmp = sb("vcmp", [NCMP, NSA_GROUPS, P], into=even)
        bias = sb("bias", [P, DG, SEQ], into=even)
        cbias = sb("cbias", [P, NSA_HEADS, NT * NCMP], into=even)
        cmask = sb("cmask", [P, NT * NCMP], into=even)
        cvalid = sb("cvalid", [P, NT, NCMP], into=even)
        pcmp, pcmp_s = sb("pcmp", [P, NT, NCMP], into=even), sb("pcmp_s", [P, NT, NCMP], into=even)
        pcmpT = sb("pcmpT", [NCMP, SEQ], into=even)
        tab = sb("tab", [BUCKETS, HEADS_B], into=even)
        rmask, rows = sb("rmask", [HEADS_B, RRW], into=even), sb("rows", [HEADS_B, RRW], into=even)
        g3w = sb("g3w", [P, KD, 24], into=even)
        g3H, g3L = sb("g3H", [P, KD, 24], f32r, even), sb("g3L", [P, KD, 24], f32r, even)
        g3z, g3t = sb("g3z", [P, NT, 24], into=even), sb("g3t", [P, NT, 24], into=even)
        g3s = sb("g3s", [P, NSA_HEADS, NT, 3], into=even)
        even.close()
        odd = ExitStack()
        latH = sb("latH", [P, KQ + KKV, SEQ], f32r, odd)
        latL = sb("latL", [P, KQ + KKV, SEQ], f32r, odd)
        probs_o = sb("probs_o", [P, 1, TW], into=odd)
        probsT_o = sb("probsT_o", [P, 1, TW], into=odd)
        v_head = sb("v_head", [P, NT, P], into=odd)
        qpe, kpe = sb("qpe", [P, MH // 2, SEQ], into=odd), sb("kpe", [P, SEQ], into=odd)
        qpc, qm, km = [sb(n, [P, SEQ], into=odd) for n in ("qpc", "qm", "km")]
        rt1, rt2 = sb("rt1", [P, SEQ], into=odd), sb("rt2", [P, SEQ], into=odd)
        cossin, cmask_m = sb("cossin", [P, 2, SEQ], into=odd), sb("cmask_m", [P, TW], into=odd)
        odd.close()
        yw = sb("yw", [P, KD, SEQ])
        PROBS = {"dil": (probs_e, probsT_e), "nsa": (probs_e, probsT_e), "mla": (probs_o, probsT_o)}

        def bank(name, banks=1):
            return ctx.enter_context(nc.psum_tensor(name, [P, banks, 512], f32))

        proj, S, PT, O, MS = bank("proj", 2), bank("S", 3), bank("PT"), bank("O"), bank("MS")

        loaded = [sem(f"piece_loaded{s}") for s in range(R)]
        x_loaded = [sem(f"x_loaded{c}") for c in range(4)]
        consts_a, consts_b, consts_odd = sem("consts_early"), sem("consts_late"), sem("consts_odd")
        rows_ready = sem("rows_ready")
        rows_stored, bias_loaded = sem("rows_stored"), sem("bias_loaded")
        w1_loaded = [sem(f"w1_loaded{s}") for s in range(2)]
        w1_used = sem("w1_used")
        stored, x_stored = sem("stored"), sem("x_stored")
        xr_loaded = [sem(f"xr_loaded{c}") for c in range(XR)]
        hi_split, lo_split, piece_used = sem("hi_split"), sem("lo_split"), sem("piece_used")
        mid_tile, tile_taken = sem("mid_tile"), sem("tile_taken")
        h_hi, h_lo, g3_hi, g3_lo = sem("h_hi"), sem("h_lo"), sem("g3_hi"), sem("g3_lo")
        x_new, lat_z, lat_hi, lat_lo = sem("x_new"), sem("lat_z"), sem("lat_hi"), sem("lat_lo")
        ms_ready, ms_taken = sem("ms_ready"), sem("ms_taken")
        inv_ready, rfac_ready = sem("inv_ready"), sem("rfac_ready")
        squares, squares_used, acc_ready = sem("squares"), sem("squares_used"), sem("acc_ready")
        scores_ready, logits_ready = sem("scores_ready"), sem("logits_ready")
        exp_ready, probs_ready = sem("exp_ready"), sem("probs_ready")
        pt_ready, pt_taken = sem("pt_ready"), sem("pt_taken")
        out_ready, out_taken = sem("out_ready"), sem("out_taken")
        mix_hi, mix_lo = sem("mix_hi"), sem("mix_lo")
        gz_ready, gt_ready = sem("gz_ready"), sem("gt_ready")
        v_copied, qp_copied = sem("v_copied"), sem("qp_copied")
        kcp_ready, cz_ready, ct_ready, cs_ready = sem("kcp_ready"), sem("cz_ready"), sem("ct_ready"), sem("cs_ready")
        g3z_ready, g3t_ready = sem("g3z_ready"), sem("g3t_ready")
        rope_z, rope_s = sem("rope_z"), sem("rope_s")
        pool_set, pool_chain, dve_chain = sem("pool_set"), sem("pool_chain"), sem("dve_chain")
        y_ready = sem("y_ready")

        block = ctx.enter_context(nc.Block())

        @block.sync
        def _(sp):
            for c in range(4):
                sp.dma_start(xT[:, 4 * c:4 * c + 4, :], x_in[:, 4 * c:4 * c + 4, :]).then_inc(x_loaded[c], 16)
                if c == 0:
                    sp.dma_start(nrm[:], norms).then_inc(consts_a, 16)
                sp.dma_start(raw[:, c, :], w_stream[c]).then_inc(loaded[c], 16)
            for dst, src in ((tab, table), (oneh, onehot), (oneh_c, onehot_cmp), (rmask, row_mask),
                             (cmask, cmp_mask), (cvalid, cmp_valid), (g3w, w_gate3), (ident, ident_in),
                             (posT, cmp_pos), (w2, w_cmp2), (qn, q_norm), (kvn, kv_norm)):
                sp.dma_start(dst[:], src).then_inc(consts_b, 16)
            for s in range(R):
                sp.wait_ge(lo_split, s + 1)
                sp.dma_start(raw[:, s, :], w_stream[R + s]).then_inc(loaded[s], 16)
            sp.wait_ge(rows_ready, 1)
            sp.dma_start(bias_rows.ap(), rows[:].rearrange("h (a n) -> h a n", a=1)
                         .to_broadcast([HEADS_B, P, RRW])).then_inc(rows_stored, 16)
            last = N_END // R
            with sp.Fori(2, last) as i:
                for s in range(R):
                    sp.wait_ge(lo_split, i * R + (s - R + 1))
                    sp.dma_start(raw[:, s, :],
                                 w_stream[ds(i * R + s, 1)].rearrange("a p n -> p (a n)")).then_inc(loaded[s], 16)
            for s in range(N_END % R):
                sp.wait_ge(lo_split, last * R + s - R + 1)
                sp.dma_start(raw[:, s, :], w_stream[last * R + s]).then_inc(loaded[s], 16)
            for c in range(4):
                sp.wait_ge(y_ready, c + 1)
                sp.dma_start(y_out[:, 4 * c:4 * c + 4, :], yw[:, 4 * c:4 * c + 4, :]).then_inc(stored, 16)
            sp.wait_ge(stored, 64)

        @block.gpsimd
        def _(pool):
            chain = Tally(pool, pool_chain)
            pool.memset(ones[:], 1.0).then_inc(pool_set, 1)
            for c in range(4):
                pool.wait_ge(x_loaded[c], 16)
                if c >= 2:
                    pool.wait_ge(squares_used, c - 1)
                xc = xT[:, 4 * c:4 * c + 4, :]
                pool.tensor_tensor(sq0[:, c % 2], xc, xc, MUL).then_inc(squares, 1)

            def copy_v_dilated(d):
                pool.wait_ge(tile_taken, T_DIL)
                for g in range(DG):
                    src = vt[:, :, ds(d * P + 512 * (g + 1), P)]
                    c = pool.tensor_copy(v_cur[:, g], src)
                c.then_inc(v_copied, 1)

            copy_v_dilated(0)
            with pool.Fori(1, DH) as d:
                pool.wait_ge(out_ready, d)
                copy_v_dilated(d)
            for m in range(2 * NSA_BLOCK // PB):
                if m >= 2:
                    pool.wait_ge(w1_used, m - 1)
                pool.dma_start(w1[:, m % 2], w_cmp1[m]).then_inc(w1_loaded[m % 2], 16)

            def add_square(k, src, first):
                chain.link(pool.tensor_tensor(sq[:, k % 2], src, src, MUL))
                if first:
                    return pool.tensor_copy(acc[:], sq[:, k % 2])
                return pool.tensor_tensor(acc[:], acc[:], sq[:, k % 2], ADD)

            for c in range(XR):
                pool.dma_start(xr[:, c], x_in[:, c]).then_inc(xr_loaded[c], 16)
            for c in range(KD):
                pool.wait_ge(x_new, c + 1)
                pool.dma_start(x_mid.ap()[:, c], xr[:, c % XR]).then_inc(x_stored, 16)
                chain.link(add_square(c, xr[:, c % XR], c == 0))
                if c + XR < KD:
                    pool.wait_ge(x_stored, 16 * (c + 1))
                    pool.wait_ge(h_lo, KD + c + 1)
                    pool.dma_start(xr[:, c % XR], x_in[:, c + XR]).then_inc(xr_loaded[c % XR], 16)
            pool.tensor_copy(nrm_sum[:], acc[:]).then_inc(acc_ready, 1)
            pool.wait_ge(x_stored, 16 * KD)
            pool.wait_ge(h_lo, 2 * KD)
            for c in range(XR):
                pool.dma_start(xr[:, c], x_mid.ap()[:, c]).then_inc(xr_loaded[c], 16)
            pool.dma_start(cossin[:], rope_cs).then_inc(consts_odd, 16)
            pool.dma_start(cmask_m[:], causal).then_inc(consts_odd, 16)
            for lo, hi in ((0, KQ), (KQ, KQ + KKV)):
                for c in range(lo, hi):
                    pool.wait_ge(lat_z, c + 1)
                    if c == lo:
                        pool.wait_ge(ms_taken, U_NORM1 + 1 if lo == 0 else U_NORMQ + 1)
                    ins = add_square(c, zt[:, c % 2], c == lo)
                    ins.then_inc(squares, 1)
                    pool.wait_ge(squares, 4 + c + 1)
                pool.tensor_copy(nrm_sum[:], acc[:]).then_inc(acc_ready, 1)

            def copy_v_mla(h):
                pool.tensor_copy(v_head[:], vt[:, :, ds(h * MV, MV)]).then_inc(v_copied, 1)

            def copy_qpe(i):
                pool.tensor_copy(qpc[:], qpe[:, ds(i, 1), :].rearrange("p a n -> p (a n)")).then_inc(qp_copied, 1)

            with pool.Fori(0, MH // 2) as i:
                pool.wait_ge(scores_ready, i * 2 + A_MLA)
                pool.wait_ge(tile_taken, T_MLA)
                copy_qpe(i)
                for b in range(2):
                    pool.wait_ge(out_ready, i * 2 + b + A_MLA)
                    pool.wait_ge(tile_taken, T_MLA)
                    copy_v_mla(i * 2 + b)
            for c in range(KD):
                pool.wait_ge(x_new, KD + c + 1)
                if c == 0:
                    pool.wait_ge(ms_taken, U_NORMKV + 1)
                ins = add_square(c, zt[:, c % 2], c == 0)
                ins.then_inc(squares, 1)
                pool.wait_ge(squares, 4 + KQ + KKV + c + 1)
                if c + XR < KD:
                    pool.dma_start(xr[:, c % XR], x_mid.ap()[:, c + XR]).then_inc(xr_loaded[c % XR], 16)
            pool.tensor_copy(nrm_sum[:], acc[:]).then_inc(acc_ready, 1)

        @block.scalar
        def _(act):
            def split(n, s, count):
                act.wait_ge(loaded[s], count * 16)
                if not isinstance(n, int) or n >= R:
                    act.wait_ge(piece_used, n - (R - 1))
                act.activation(wH[:, s], raw[:, s], ACT.Copy).then_inc(hi_split, 1)

            def split_at(n):
                if n < N_END:
                    split(n, n % R, n // R + 1)

            def split_in(n0, i, per, j):
                m = n0 + j
                split(i * per + m, m % R, i * (per // R) + (m // R + 1))

            def gate_tanh(a):
                act.wait_ge(gz_ready, a + 1)
                act.activation(gate_t[:], gate_z[:], ACT.Tanh, scale=0.5).then_inc(gt_ready, 1)

            def exps(a, kind):
                act.wait_ge(logits_ready, a + 1)
                probs = PROBS[kind][0]
                if kind == "dil":
                    for t in range(NT):
                        v = probs[:, :, 0:P] if t == 0 else probs[:, :, P:TW]
                        e = act.activation(v, v, ACT.Exp, bias=nmx[:, t, 0:1], scale=SC_EVEN,
                                           accum_out=den[:, t, 0:1])
                if kind == "nsa":
                    act.activation(pcmp[:], pcmp[:], ACT.Exp, scale=SC_EVEN)
                if kind in ("nsa", "mla"):
                    for g in range(2 if kind == "nsa" else 1):
                        for t in range(NT):
                            v = probs[:, g, 0:P] if t == 0 else probs[:, g, P:TW]
                            col = g + 1 if kind == "nsa" else 0
                            e = act.activation(v, v, ACT.Exp, bias=nmx[:, t, col:col + 1],
                                               scale=SC_EVEN if kind == "nsa" else SC_MLA,
                                               accum_out=den[:, t, col:col + 1])
                e.then_inc(exp_ready, 1)

            def take_pt(k, g, kind):
                act.wait_ge(pt_ready, k + 1)
                if kind == "cmp":
                    act.activation(pcmpT[:], S[0:NCMP, 2, P:P + SEQ], ACT.Copy).then_inc(pt_taken, 1)
                else:
                    act.activation(PROBS[kind][1][:, g], PT[:, 0, 0:TW], ACT.Copy).then_inc(pt_taken, 1)

            def mix_high(a, idx):
                act.wait_ge(out_taken, a + 1)
                out = mixH[:, idx] if isinstance(idx, int) else mixH[:, ds(idx, 1), :].rearrange("p a n -> p (a n)")
                act.activation(out, mixf[:], ACT.Copy).then_inc(mix_hi, 1)

            def load_bias(a, row0, step, n):
                if not isinstance(a, int) or a > 0:
                    act.wait_ge(logits_ready, a)
                act.wait_ge(rows_stored, 16)
                for g in range(n):
                    r = row0 + g * step
                    src = bass.AP(bias_rows, r * (P * RRW) + (P - 1), [[RRW - 1, P], [1, SEQ]])
                    act.dma_start(bias[:, g, :], src).then_inc(bias_loaded, 16)

            def slot_ops(j, a, idx, kind, g0):
                if j == 0:
                    gate_tanh(a)
                    exps(a, kind)
                    if kind == "dil" and isinstance(a, int) and a == DH - 1:
                        load_bias(A_NSA, 0, 0, 1)
                if kind == "dil":
                    if 3 <= j <= 5:
                        take_pt(g0 + j - 3, j - 3, kind)
                    if j == 6:
                        mix_high(a, idx)
                if kind == "nsa":
                    if j == 2:
                        take_pt(g0, 0, kind)
                        take_pt(g0 + 1, 0, "cmp")
                    if j == 3:
                        take_pt(g0 + 2, 1, kind)
                        mix_high(a, idx)
                if kind == "mla":
                    if j == 2:
                        take_pt(g0, 0, kind)
                    if j == 3:
                        mix_high(a, idx)

            act.wait_ge(consts_a, 16)
            for c in range(KD):
                act.wait_ge(x_loaded[c // 4], 16)
                act.activation(hH[:, c], xT[:, c], ACT.Copy, scale=nrm[:, 0, c:c + 1]).then_inc(h_hi, 1)
                if c % 4 == 3 and c // 4 < LEAD:
                    split_at(c // 4)
            act.wait_ge(consts_b, 16 * 12)
            act.activation(g3H[:], g3w[:], ACT.Copy).then_inc(g3_hi, 1)
            for j in range(PB):
                split_at(j + LEAD)
                if j == 4:
                    act.wait_ge(inv_ready, 1)
                    act.activation(rfac[:], rtmp[:], ACT.Sqrt).then_inc(rfac_ready, 1)
                if j == 7:
                    act.wait_ge(g3z_ready, 1)
                    act.activation(g3t[:], g3z[:], ACT.Tanh, scale=0.5).then_inc(g3t_ready, 1)
            load_bias(0, NSA_HEADS, DH, DG)
            with act.Fori(1, 4) as i:
                for j in range(PB):
                    split_in(N_V, i, PB, j + LEAD)
            for j in range(16):
                split_at(N_DIL + j + LEAD)
            with act.Fori(1, DH) as d:
                for j in range(16):
                    split_in(N_DIL, d, 16, j + LEAD)
                    slot_ops(j, d - 1, d + (NSA_HEADS - 1), "dil", (d - 1) * DG)
                    if j == 0:
                        load_bias(d, d + NSA_HEADS, DH, DG)
            for j in range(8):
                split_at(N_KSW + j + LEAD)
                slot_ops(j, DH - 1, NSA_HEADS + DH - 1, "dil", (DH - 1) * DG)
            act.wait_ge(cz_ready, 1)
            act.activation(ct[:], cz[:], ACT.Tanh, scale=0.5).then_inc(ct_ready, 1)
            for j in range(4):
                split_at(N_NSA + j + LEAD)
            with act.Fori(1, NSA_HEADS) as h:
                for j in range(4):
                    split_in(N_NSA, h, 4, j + LEAD)
                    slot_ops(j, h + (A_NSA - 1), h - 1, "nsa", (h - 1) * 3 + G_NSA)
                    if j == 0:
                        load_bias(h + A_NSA, h, 0, 1)
            tile = 0
            for j in range(KD * EVEN_MIX // PB):
                split_at(N_WOE + j + LEAD)
                if j < 4:
                    slot_ops(j, A_MLA - 1, NSA_HEADS - 1, "nsa", G_MLA - 3)
                while tile < KD and woe_end(tile) < (j + 1) * PB:
                    act.wait_ge(x_new, tile + 1)
                    act.activation(hH[:, tile], xr[:, tile % XR], ACT.Copy,
                                   scale=nrm[:, 1, tile:tile + 1]).then_inc(h_hi, 1)
                    tile += 1

            def latent_high(c):
                act.wait_ge(lat_z, c + 1)
                out = latH[:, c] if isinstance(c, int) else latH[:, ds(c, 1), :].rearrange("p a n -> p (a n)")
                return out

            def latent_pair(n0, i, c0):
                for j in range(4):
                    if isinstance(i, int):
                        split_at(n0 + i * 4 + j + LEAD)
                    else:
                        split_in(n0, i, 4, j + LEAD)
                    if j % 2:
                        out = latent_high(i * 2 + c0 + j // 2)
                        act.activation(out, zw[:, j // 2], ACT.Copy).then_inc(lat_hi, 1)

            def root(k, dst):
                act.wait_ge(inv_ready, k)
                act.activation(dst[:], rtmp[:], ACT.Sqrt).then_inc(rfac_ready, 1)

            for j in range(4):
                split_at(N_LAT + j + LEAD)
                if j == 1:
                    root(2, rfac)
                if j % 2:
                    act.activation(latent_high(j // 2), zw[:, j // 2], ACT.Copy).then_inc(lat_hi, 1)
            with act.Fori(1, KQ // 2) as i:
                latent_pair(N_LAT, i, 0)
            nkv = N_LAT + 2 * KQ
            for j in range(2 * KKV):
                split_at(nkv + j + LEAD)
                if j == 2:
                    root(3, rq)
                if j % 2:
                    act.activation(latent_high(KQ + j // 2), zw[:, (j // 2) % 2], ACT.Copy).then_inc(lat_hi, 1)

            def swap_halves(k):
                act.wait_ge(rope_z, k)
                for q in range(4):
                    c = act.activation(zs[32 * q:32 * q + 32], zt[32 * (q ^ 1):32 * (q ^ 1) + 32, 0], ACT.Copy)
                c.then_inc(rope_s, 1)

            for j in range(2):
                split_at(nkv + 2 * KKV + j + LEAD)
                if j == 1:
                    root(4, rkv)
                    swap_halves(1)
            for j in range(N_VM - N_PE):
                split_at(N_PE + j + LEAD)
                for m in range(pe_tiles_ending(j)[0], pe_tiles_ending(j)[1]):
                    swap_halves(2 + m)
            for j in range(N_MLA - N_VM):
                split_at(N_VM + j + LEAD)

            def mla_pair(i, first):
                for b in range(2):
                    for j in range(4):
                        if isinstance(i, int):
                            split_at(N_MLA + i * 8 + b * 4 + j + LEAD)
                        else:
                            split_in(N_MLA, i, 8, b * 4 + j + LEAD)
                        if not (first and b == 0):
                            slot_ops(j, i * 2 + (b + A_MLA - 1), i * 2 + (b - 1), "mla", i * 2 + (b + G_MLA - 1))

            mla_pair(0, True)
            with act.Fori(1, MH // 2) as i:
                mla_pair(i, False)
            for j in range(4):
                split_at(N_WOO + j + LEAD)
                slot_ops(j, A_MLA + MH - 1, MH - 1, "mla", G_MLA + MH - 1)
            with act.Fori(1, KD // 2 - 1) as i:
                for j in range(4):
                    split_in(N_WOO, i, 4, j + LEAD)
            for j in range(4):
                split_at(N_END - 4 + j + LEAD)
            root(5, rfac)

        @block.vector
        def _(dve):
            chain = Tally(dve, dve_chain)
            link = chain.link

            marks = {}

            def mark(s):
                col = marks.setdefault(s.name, len(marks))
                dve.memset(tick[:, col:col + 1], 0.0).then_inc(s, 1)

            def split(n, s):
                dve.wait_ge(hi_split, n + 1)
                dve.tensor_tensor(wL[:, s], raw[:, s], wH[:, s].bitcast(f32), SUB).then_inc(lo_split, 1)

            def split_at(n):
                if n < N_END:
                    split(n, n % R)

            def split_in(n0, i, per, j):
                split(i * per + (n0 + j), (n0 + j) % R)

            def take_tile(out, t, factor):
                dve.tensor_tensor(out, proj[:, t % 2, 0:SEQ], factor, MUL).then_inc(tile_taken, 1)

            RF = rfac[:, 0:SEQ]

            def take_gate(t):
                take_tile(gate_z[:], t, RF)
                mark(gz_ready)

            def add_max(out, a, b, top):
                return dve.tensor_tensor_reduce(out=out, in0=a, in1=b, scale=1.0, scalar=-3.0e38,
                                                op0=ADD, op1=MAX, accum_out=top)

            def logits(a, kind, h=None):
                dve.wait_ge(scores_ready, a + 1)
                probs = PROBS[kind][0]
                if kind != "mla":
                    first = 16 * DG
                    want = (a + 1) * first if kind == "dil" else a * 16 + 16 * (DH * DG - DH + 1)
                    dve.wait_ge(bias_loaded, want)
                dve.memset(tick[:, 15:16], 0.0)
                if kind == "dil":
                    for g in range(DG):
                        add_max(probs[:, g, 0:P], S[:, g, 0:P], bias[:, g, P:SEQ], mx[:, 0, g:g + 1])
                        top = add_max(probs[:, g, P:TW], S[:, g, P:TW], bias[:, g, :], mx[:, 1, g:g + 1])
                    link(top)
                    link(dve.tensor_reduce(mx1[:], mx[:], AX.X, MAX))
                    dve.tensor_scalar(nmx[:, :, 0], mx1[:], -SC_EVEN, None, MUL).then_inc(logits_ready, 1)
                if kind == "nsa":
                    for g in range(2):
                        add_max(probs[:, g, 0:P], S[:, g, 0:P], bias[:, 0, P:SEQ], mx[:, 0, g + 1:g + 2])
                        add_max(probs[:, g, P:TW], S[:, g, P:TW], bias[:, 0, :], mx[:, 1, g + 1:g + 2])
                    cb = cbias[:, h] if isinstance(h, int) else cbias[:, ds(h, 1), :].rearrange("p a n -> p (a n)")
                    link(dve.tensor_tensor(pcmp[:].rearrange("p t n -> p (t n)"), S[:, 2, 0:NT * NCMP], cb, ADD))
                    link(dve.tensor_reduce(mx[:, :, 0], pcmp[:], AX.X, MAX))
                    dve.tensor_scalar(nmx[:], mx[:], -SC_EVEN, None, MUL)
                    for t in range(NT):
                        c = dve.tensor_scalar(pcmp[:, t], pcmp[:, t], mx[:, t, 0:1], None, SUB)
                    c.then_inc(logits_ready, 1)
                if kind == "mla":
                    add_max(probs[:, 0, 0:P], S[:, 0, 0:P], cmask_m[:, 0:P], mx[:, 0, 0:1])
                    link(add_max(probs[:, 0, P:TW], S[:, 0, P:TW], cmask_m[:, P:TW], mx[:, 1, 0:1]))
                    dve.tensor_scalar(nmx[:, :, 0], mx[:, :, 0], -SC_MLA, None, MUL).then_inc(logits_ready, 1)

            def scale_probs(a, kind, h=None):
                dve.wait_ge(exp_ready, a + 1)
                probs = PROBS[kind][0]
                if kind == "dil":
                    link(dve.reciprocal(coef[:, :, 0], den[:, :, 0]))
                    dve.tensor_scalar(probs[:, :, 0:P], probs[:, :, 0:P], coef[:, 0, 0:1], None, MUL)
                    dve.tensor_scalar(probs[:, :, P:TW], probs[:, :, P:TW], coef[:, 1, 0:1], None,
                                      MUL).then_inc(probs_ready, 1)
                if kind == "nsa":
                    link(dve.tensor_reduce(den[:, :, 0], pcmp[:], AX.X, ADD))
                    link(dve.reciprocal(coef[:], den[:]))
                    gs = g3s[:, h] if isinstance(h, int) else g3s[:, ds(h, 1)].rearrange("p a t g -> p (a t) g")
                    link(dve.tensor_tensor(coef[:], coef[:], gs, MUL))
                    for t in range(NT):
                        dve.scalar_tensor_tensor(pcmp_s[:, t], pcmp[:, t], coef[:, t, 0:1], cvalid[:, t], MUL, MUL)
                    for g in range(2):
                        dve.tensor_scalar(probs[:, g, 0:P], probs[:, g, 0:P], coef[:, 0, g + 1:g + 2], None, MUL)
                        c = dve.tensor_scalar(probs[:, g, P:TW], probs[:, g, P:TW],
                                              coef[:, 1, g + 1:g + 2], None, MUL)
                    c.then_inc(probs_ready, 1)
                if kind == "mla":
                    link(dve.reciprocal(coef[:, :, 0], den[:, :, 0]))
                    dve.tensor_scalar(probs[:, 0, 0:P], probs[:, 0, 0:P], coef[:, 0, 0:1], None, MUL)
                    dve.tensor_scalar(probs[:, 0, P:TW], probs[:, 0, P:TW], coef[:, 1, 0:1], None,
                                      MUL).then_inc(probs_ready, 1)

            def gate_silu(a):
                dve.wait_ge(gt_ready, a + 1)
                link(dve.scalar_tensor_tensor(gate_g[:], gate_t[:], 1.0, gate_z[:], ADD, MUL))

            def mix(a):
                dve.wait_ge(out_ready, a + 1)
                dve.scalar_tensor_tensor(mixf[:], O[:, 0, 0:SEQ], 0.5, gate_g[:], MUL, MUL).then_inc(out_taken, 1)

            def mix_low(a, idx):
                dve.wait_ge(mix_hi, a + 1)
                if isinstance(idx, int):
                    hi, lo = mixH[:, idx], mixL[:, idx]
                else:
                    hi = mixH[:, ds(idx, 1), :].rearrange("p a n -> p (a n)")
                    lo = mixL[:, ds(idx, 1), :].rearrange("p a n -> p (a n)")
                dve.tensor_tensor(lo, mixf[:], hi.bitcast(f32), SUB).then_inc(mix_lo, 1)

            def slot_ops(j, a, idx, kind, h=None):
                if j == 0:
                    logits(a, kind, h)
                if j == 1:
                    scale_probs(a, kind, h)
                    gate_silu(a)
                if kind == "dil":
                    if j == 6:
                        mix(a)
                    if j == 7:
                        mix_low(a, idx)
                elif j == 3:
                    mix(a)
                    mix_low(a, idx)

            def refine(dst, k):
                dve.wait_ge(rfac_ready, k)
                link(dve.tensor_tensor(rnew[:], dst[:], dst[:], MUL))
                link(dve.tensor_tensor(rnew[:], rnew[:], rvar[:], MUL))
                link(dve.tensor_scalar(rnew[:], rnew[:], -0.5, 1.5, MUL, ADD))
                link(dve.tensor_tensor(dst[:], dst[:], rnew[:], MUL))

            def take_norm(use, k, n):
                dve.wait_ge(ms_ready, use + 1)
                if k > 1:
                    dve.wait_ge(rfac_ready, k - 1)
                if use == U_NORM0:
                    dve.tensor_scalar(rvar[:, SEQ:], S[:, 0:NT, 0], 1.0 / n, EPS, MUL, ADD)
                    link(dve.tensor_scalar(rvar[:, 0:SEQ], MS[:, 0, 0:SEQ], 1.0 / n, EPS, MUL, ADD))
                else:
                    link(dve.tensor_scalar(rvar[:], MS[:, 0, 0:SEQ + NT], 1.0 / n, EPS, MUL, ADD))
                mark(ms_taken)
                dve.reciprocal(rtmp[:], rvar[:]).then_inc(inv_ready, 1)

            for c in range(KD):
                dve.wait_ge(h_hi, c + 1)
                dve.scalar_tensor_tensor(hL[:, c], xT[:, c], nrm[:, 0, c:c + 1], hH[:, c].bitcast(f32),
                                         MUL, SUB).then_inc(h_lo, 1)
                if c % 4 == 3 and c // 4 < LEAD:
                    split_at(c // 4)
            dve.wait_ge(g3_hi, 1)
            dve.tensor_tensor(g3L[:], g3w[:], g3H[:].bitcast(f32), SUB).then_inc(g3_lo, 1)
            dve.wait_ge(ms_ready, U_BIAS + 1)
            link(dve.scalar_tensor_tensor(rows[:], MS[0:HEADS_B, 0, 0:RRW], ROOT, rmask[:], MUL, ADD))
            mark(ms_taken)
            mark(rows_ready)

            def take_values(c):
                for t in range(NT):
                    out = (vt[:, t, c * 512:(c + 1) * 512] if isinstance(c, int) else vt[:, t, ds(c * 512, 512)])
                    dve.tensor_scalar(out, proj[:, t, :], rfac[:, SEQ + t:SEQ + t + 1], None,
                                      MUL).then_inc(tile_taken, 1)

            for j in range(PB):
                split_at(j + LEAD)
                if j == 1:
                    dve.wait_ge(ms_ready, U_CBIAS + 1)
                    psum = MS[:, 0, 0:64].rearrange("p (t h) -> p h t", h=NSA_HEADS)
                    msk = cmask[:].rearrange("p (a t) -> p a t", a=1).to_broadcast([P, NSA_HEADS, NT * NCMP])
                    dve.scalar_tensor_tensor(cbias[:], psum, ROOT, msk, MUL, ADD).then_inc(ms_taken, 1)
                if j == 4:
                    take_norm(U_NORM0, 1, D_MODEL)
                if j == 6:
                    dve.wait_ge(ms_ready, U_GATE3 + 1)
                    refine(rfac, 1)
                    for t in range(NT):
                        c = dve.tensor_scalar(g3z[:, t], MS[:, 0, 24 * t:24 * t + 24],
                                              rfac[:, SEQ + t:SEQ + t + 1], None, MUL)
                    link(c)
                    mark(ms_taken)
                    mark(g3z_ready)
            dve.wait_ge(g3t_ready, 1)
            for t in range(NT):
                dve.tensor_scalar(g3s[:, :, t, :], g3t[:, t].rearrange("p (h b) -> p h b", b=3), 1.0, 0.5, ADD, MUL)
            dve.wait_ge(piece_used, PB)
            take_values(0)
            with dve.Fori(1, 4) as i:
                for j in range(PB):
                    split_in(N_V, i, PB, j + LEAD)
                dve.wait_ge(piece_used, i * PB + PB)
                take_values(i)

            def dilated(d, attend):
                for j in range(16):
                    if attend:
                        slot_ops(j, d - 1, d + (NSA_HEADS - 1), "dil")
                        split_in(N_DIL, d, 16, j + LEAD)
                    else:
                        split_at(N_DIL + j + LEAD)
                    if j % 2:
                        t = j // 2
                        dve.wait_ge(piece_used, d * 16 + (N_DIL + j + 1))
                        if t < 3:
                            take_tile(qd[:, t], t, RF)
                        elif t < 6:
                            take_tile(kd[:, t - 3], t, RF)
                        elif t == 6:
                            out = kvc[:, d] if isinstance(d, int) else kvc[:, ds(d, 1), :].rearrange("p a n -> p (a n)")
                            take_tile(out, t, RF)
                        else:
                            take_gate(t)

            dilated(0, False)
            with dve.Fori(1, DH) as d:
                chain.turn(d - 1, DVE_TURN["dil"])
                dilated(d, True)
            chain.leave(DH - 1)
            for j in range(8):
                if j == 0:
                    dve.wait_ge(tile_taken, T_KSW)
                    for w in range(2):
                        for g in range(NSA_GROUPS):
                            src = kvc[:, 2 * w + g].rearrange("p (n s) -> p s n", s=NSA_BLOCK)
                            pos = posT[:, w].rearrange("p (s a) -> p s a", a=1).to_broadcast([P, NSA_BLOCK, NCMP])
                            c = dve.tensor_tensor(kcp[:, w, :, g * NCMP:(g + 1) * NCMP], src, pos, ADD)
                    c.then_inc(kcp_ready, 1)
                slot_ops(j, DH - 1, NSA_HEADS + DH - 1, "dil")
                split_at(N_KSW + j + LEAD)
                if j % 2:
                    dve.wait_ge(piece_used, N_KSW + j + 1)
                    take_tile(ksw[:, j // 2], j // 2, RF)
            dve.wait_ge(ms_ready, U_CMP + 1)
            link(dve.tensor_copy(cz[:].rearrange("p w n -> p (w n)"), MS[:, 0, 0:16]))
            mark(ms_taken)
            mark(cz_ready)
            dve.wait_ge(ct_ready, 1)
            link(dve.scalar_tensor_tensor(cs[:], ct[:], 1.0, cz[:], ADD, MUL))
            dve.tensor_scalar(cs[:], cs[:], 0.5, None, MUL).then_inc(cs_ready, 1)

            def nsa(h, attend):
                for j in range(4):
                    if not attend and j == 2:
                        dve.wait_ge(ms_ready, U_CMP2 + 1)
                        dve.tensor_copy(kcmp[:], MS[:, 0, 0:8])
                        for g in range(NSA_GROUPS):
                            c = dve.tensor_copy(vcmp[:, g], MS[0:NCMP, 0, P * (g + 1):P * (g + 2)])
                        c.then_inc(ms_taken, 1)
                    if attend:
                        slot_ops(j, h + (A_NSA - 1), h - 1, "nsa", h - 1)
                        split_in(N_NSA, h, 4, j + LEAD)
                    else:
                        split_at(N_NSA + j + LEAD)
                    if j % 2:
                        dve.wait_ge(piece_used, h * 4 + (N_NSA + j + 1))
                        if j == 1:
                            take_tile(qa[:], 0, RF)
                        else:
                            take_gate(1)

            nsa(0, False)
            with dve.Fori(1, NSA_HEADS) as h:
                chain.turn(h - 1, DVE_TURN["nsa"])
                nsa(h, True)
            chain.leave(NSA_HEADS - 1)

            tile = 0
            for j in range(KD * EVEN_MIX // PB):
                if j < 4:
                    slot_ops(j, A_MLA - 1, NSA_HEADS - 1, "nsa", NSA_HEADS - 1)
                split_at(N_WOE + j + LEAD)
                while tile < KD and woe_end(tile) < (j + 1) * PB:
                    mid = woe_mid(tile)
                    if mid is None:
                        dve.wait_ge(piece_used, N_WOE + j + 1)
                    else:
                        dve.wait_ge(mid_tile, mid + 1)
                    src = S[:, 1, 0:SEQ] if tile == 2 else proj[:, (T_WOE + tile) % 2, 0:SEQ]
                    xc = xr[:, tile % XR]
                    dve.wait_ge(xr_loaded[tile % XR], 16 * (tile // XR + 1))
                    link(dve.tensor_tensor(xc, xc, src, ADD))
                    mark(tile_taken)
                    mark(x_new)
                    dve.wait_ge(h_hi, KD + tile + 1)
                    dve.scalar_tensor_tensor(hL[:, tile], xc, nrm[:, 1, tile:tile + 1],
                                             hH[:, tile].bitcast(f32), MUL, SUB).then_inc(h_lo, 1)
                    tile += 1

            def latent(c, t, par, weight):
                if not isinstance(c, int) or c >= 2:
                    dve.wait_ge(squares, c + 3)
                link(dve.tensor_tensor(zt[:, par], proj[:, t % 2, 0:SEQ], RF, MUL))
                link(dve.tensor_scalar(zw[:, par], zt[:, par], weight, None, MUL))
                mark(tile_taken)
                mark(lat_z)
                dve.wait_ge(lat_hi, c + 1)
                if isinstance(c, int):
                    hi, lo = latH[:, c], latL[:, c]
                else:
                    hi = latH[:, ds(c, 1), :].rearrange("p a n -> p (a n)")
                    lo = latL[:, ds(c, 1), :].rearrange("p a n -> p (a n)")
                dve.tensor_tensor(lo, zw[:, par], hi.bitcast(f32), SUB).then_inc(lat_lo, 1)

            for j in range(4):
                split_at(N_LAT + j + LEAD)
                if j == 1:
                    take_norm(U_NORM1, 2, D_MODEL)
                    refine(rfac, 2)
                if j % 2:
                    dve.wait_ge(piece_used, N_LAT + j + 1)
                    latent(j // 2, T_LAT + j // 2, j // 2, qn[:, j // 2:j // 2 + 1])
            with dve.Fori(1, KQ // 2) as i:
                chain.turn(i - 1, DVE_TURN["lat"])
                for j in range(4):
                    split_in(N_LAT, i, 4, j + LEAD)
                    if j % 2:
                        dve.wait_ge(piece_used, i * 4 + (N_LAT + j + 1))
                        c = i * 2 + j // 2
                        latent(c, T_LAT + j // 2, j // 2, qn[:, ds(c, 1)])
            chain.leave(KQ // 2 - 1)
            nkv, tkv = N_LAT + 2 * KQ, T_LAT + KQ
            for j in range(2 * KKV):
                split_at(nkv + j + LEAD)
                if j == 2:
                    take_norm(U_NORMQ, 3, QR)
                if j == 4:
                    refine(rq, 3)
                if j % 2:
                    c = j // 2
                    dve.wait_ge(piece_used, nkv + j + 1)
                    latent(KQ + c, tkv + c, c % 2, kvn[:, c:c + 1])

            def rotate(out, t, factor, k):
                if k == 1:
                    dve.wait_ge(squares, 4 + KQ + KKV)
                link(dve.tensor_tensor(zt[:, 0], proj[:, t % 2, 0:SEQ], factor, MUL))
                mark(tile_taken)
                mark(rope_z)
                dve.tensor_tensor(rt1[:], zt[:, 0], cossin[:, 0], MUL)
                dve.wait_ge(rope_s, k)
                link(dve.tensor_tensor(rt2[:], zs[:], cossin[:, 1], MUL))
                return dve.tensor_tensor(out, rt1[:], rt2[:], ADD)

            dve.wait_ge(consts_odd, 32)
            for j in range(2):
                split_at(nkv + 2 * KKV + j + LEAD)
                if j == 1:
                    take_norm(U_NORMKV, 4, KVR)
                    dve.wait_ge(piece_used, nkv + 2 * KKV + 2)
                    link(rotate(kpe[:], T_LAT + KQ + KKV, RF, 1))
            for j in range(N_VM - N_PE):
                split_at(N_PE + j + LEAD)
                lo, hi = pe_tiles_ending(j)
                for m in range(lo, hi):
                    if m % 2 == 0:
                        dve.wait_ge(mid_tile, MID_PE + m // 2 + 1)
                    else:
                        dve.wait_ge(piece_used, N_PE + j + 1)
                    link(rotate(qpe[:, m], T_PE + m, rq[:, 0:SEQ], 2 + m))
            refine(rkv, 4)
            for j in range(8):
                split_at(N_VM + j + LEAD)
                if j % 2:
                    dve.wait_ge(piece_used, N_VM + j + 1)
                    for t in range(NT):
                        dve.tensor_scalar(vt[:, t, 512 * (j // 2):512 * (j // 2) + 512],
                                          proj[:, (T_VM + t) % 2, :], rkv[:, SEQ + t:SEQ + t + 1], None,
                                          MUL).then_inc(tile_taken, 1)

            def mla_pair(i, first):
                for b in range(2):
                    for j in range(4):
                        jj = b * 4 + j
                        if not (first and b == 0):
                            slot_ops(j, i * 2 + (b + A_MLA - 1), i * 2 + (b - 1), "mla")
                        if isinstance(i, int):
                            split_at(N_MLA + i * 8 + jj + LEAD)
                        else:
                            split_in(N_MLA, i, 8, jj + LEAD)
                        t = T_MLA + 3 * b
                        if j == 1:
                            dve.wait_ge(mid_tile, i * 2 + (b + MID_MLA + 1))
                            take_tile(qm[:], t, rq[:, 0:SEQ])
                            dve.wait_ge(piece_used, i * 8 + (N_MLA + jj + 1))
                            take_tile(km[:], t + 1, rkv[:, 0:SEQ])
                        if j == 3:
                            dve.wait_ge(piece_used, i * 8 + (N_MLA + jj + 1))
                            take_gate(t + 2)

            mla_pair(0, True)
            with dve.Fori(1, MH // 2) as i:
                chain.turn(i - 1, DVE_TURN["mla"])
                mla_pair(i, False)
            chain.leave(MH // 2 - 1)

            def last_residual(c, s, par, t):
                if not isinstance(c, int) or c >= 2:
                    dve.wait_ge(squares, c + (3 + KQ + KKV))
                if isinstance(c, int):
                    yc, nw = yw[:, c], nrm[:, 2, c:c + 1]
                else:
                    yc, nw = yw[:, ds(c, 1), :].rearrange("p a n -> p (a n)"), nrm[:, 2, ds(c, 1)]
                link(dve.tensor_tensor(zt[:, par], xr[:, s], proj[:, t % 2, 0:SEQ], ADD))
                mark(tile_taken)
                mark(x_new)
                link(dve.tensor_scalar(yc, zt[:, par], nw, None, MUL))

            for j in range(4):
                slot_ops(j, A_MLA + MH - 1, MH - 1, "mla")
                split_at(N_WOO + j + LEAD)
            dve.wait_ge(mid_tile, MID_WOO + 1)
            dve.wait_ge(xr_loaded[0], 16 * (KD // XR + 1))
            last_residual(0, 0, 0, T_WOO)
            dve.wait_ge(piece_used, N_WOO + 4)
            dve.wait_ge(xr_loaded[1], 16 * (KD // XR + 1))
            last_residual(1, 1, 1, T_WOO + 1)

            for j in range(4):
                split_at(N_WOO + 4 + j + LEAD)
                if j % 2:
                    c = 2 + j // 2
                    dve.wait_ge(piece_used, N_WOO + 4 + j + 1)
                    dve.wait_ge(xr_loaded[c], 16 * (KD // XR + 1))
                    last_residual(c, c, c % 2, T_WOO + c)
            with dve.Fori(1, KD // XR - 1) as i:
                chain.turn(i - 1, DVE_TURN["woo"])
                for j in range(8):
                    split_in(N_WOO, i, 8, j + LEAD)
                    if j % 2:
                        c = j // 2
                        dve.wait_ge(piece_used, i * 8 + (N_WOO + j + 1))
                        dve.wait_ge(xr_loaded[c], i * 16 + 16 * (KD // XR + 1))
                        last_residual(i * 4 + c, c, c % 2, T_WOO + c)
            chain.leave(KD // XR - 2)
            for j in range(8):
                split_at(N_END - 8 + j + LEAD)
                if j % 2:
                    c = KD - 4 + j // 2
                    dve.wait_ge(piece_used, N_END - 8 + j + 1)
                    dve.wait_ge(xr_loaded[c % XR], 16 * (KD // XR + c // XR + 1))
                    last_residual(c, c % XR, c % 2, T_WOO + c)
            take_norm(U_NORMF, 5, D_MODEL)
            refine(rfac, 5)
            for c in range(4):
                xc = yw[:, 4 * c:4 * c + 4, :]
                fac = rfac[:, 0:SEQ].rearrange("p (a n) -> p a n", a=1).to_broadcast([P, 4, SEQ])
                dve.tensor_tensor(xc, xc, fac, MUL).then_inc(y_ready, 1)

        @block.tensor
        def _(pe):
            def piece(b, n, s):
                if b % PB == 0:
                    pe.wait_ge(lo_split, n + 1)
                cols = slice((b % PB) * P, (b % PB + 1) * P)
                return wH[:, s, cols], wL[:, s, cols]

            def products(out, WH, WL, aH, aL, start, stop):
                pe.matmul(out, WH, aH, start=start, stop=False)
                pe.matmul(out, WH, aL, start=False, stop=False)
                return pe.matmul(out, WL, aH, start=False, stop=stop)

            def done(last, b, mid=False):
                if b % PB == PB - 1:
                    last.then_inc(piece_used, 1)
                elif mid:
                    last.then_inc(mid_tile, 1)

            def tile_part(out, b0, n0, i, per, aH, aL, order, first=True, final=True, ready=None):
                for k, src in enumerate(order):
                    b = b0 + k
                    n = n0 + b // PB
                    if ready is not None:
                        ready(src)
                    WH, WL = piece(b, i * per + n, n % R)
                    stop = final and k == len(order) - 1
                    last = products(out, WH, WL, aH[:, src], aL[:, src], first and k == 0, stop)
                    done(last, b, stop)

            def tile_free(t):
                pe.wait_ge(tile_taken, t - 1)

            def full(t, par, b0, n0, i, per, aH, aL, count, ready=None):
                tile_free(t)
                tile_part(proj[:, par % 2, 0:SEQ], b0, n0, i, per, aH, aL, range(count), ready=ready)

            def values(t, b0, n0, i, per, aH, aL, count, par=0, ready=None, between=None):
                tile_free(t + 1)
                for k in range(count):
                    b = b0 + 4 * k
                    n = n0 + b // PB
                    if ready is not None:
                        ready(k)
                    if b % PB == 0:
                        pe.wait_ge(lo_split, i * per + (n + 1))
                    s, half = n % R, slice((b % PB) * P, (b % PB + 4) * P)
                    for tt in range(NT):
                        toks = slice(tt * P, (tt + 1) * P)
                        out = proj[:, (par + tt) % 2, :]
                        pe.matmul(out, aH[:, k, toks], wH[:, s, half], start=k == 0, stop=False)
                        pe.matmul(out, aL[:, k, toks], wH[:, s, half], start=False, stop=False)
                        last = pe.matmul(out, aH[:, k, toks], wL[:, s, half], start=False, stop=k == count - 1)
                    if b % PB == 4:
                        last.then_inc(piece_used, 1)
                        if between is not None:
                            between(k // 2)

            def norm_sums(use, k):
                pe.wait_ge(acc_ready, k)
                pe.wait_ge(ms_taken, use)
                pe.matmul(MS[:, 0, 0:SEQ], ones[:], nrm_sum[:], start=True, stop=True)
                for t in range(NT):
                    last = pe.matmul(MS[:, 0, SEQ + t:SEQ + t + 1], nrm_sum[:, t * P:(t + 1) * P],
                                     ones[:, 0:1], start=True, stop=True)
                last.then_inc(ms_ready, 1)

            def start_up(j):
                if j == 0:
                    pe.wait_ge(consts_b, 16 * 12)
                    pe.matmul(MS[0:HEADS_B, 0, 0:RRW], tab[:], oneh[:], start=True, stop=True).then_inc(ms_ready, 1)
                if j == 1:
                    pe.wait_ge(ms_taken, U_CBIAS)
                    for tn in range(NT * NCMP):
                        last = pe.matmul(MS[:, 0, tn * 8:tn * 8 + 8], oneh_c[:, tn], tab[:, 0:NSA_HEADS],
                                         start=True, stop=True)
                    last.then_inc(ms_ready, 1)
                if j == 3:
                    pe.wait_ge(ms_taken, U_NORM0)
                    for half in range(4):
                        pe.wait_ge(squares, half + 1)
                        for c in range(4):
                            k = half * 4 + c
                            last = pe.matmul(MS[:, 0, 0:SEQ], ones[:], sq0[:, half % 2, c], start=k == 0, stop=k == KD - 1)
                            for t in range(NT):
                                last = pe.matmul(S[:, t, 0:1], sq0[:, half % 2, c, t * P:(t + 1) * P],
                                                 ones[:, 0:1], start=k == 0, stop=k == KD - 1)
                        last.then_inc(squares_used if half < 3 else ms_ready, 1)
                if j == 5:
                    pe.wait_ge(ms_taken, U_GATE3)
                    pe.wait_ge(g3_lo, 1)
                    for t in range(NT):
                        toks = slice(t * P, (t + 1) * P)
                        for k in range(KD):
                            out = MS[:, 0, 24 * t:24 * t + 24]
                            pe.matmul(out, hH[:, k, toks], g3H[:, k], start=k == 0, stop=False)
                            pe.matmul(out, hL[:, k, toks], g3H[:, k], start=False, stop=False)
                            last = pe.matmul(out, hH[:, k, toks], g3L[:, k], start=False, stop=k == KD - 1)
                    last.then_inc(ms_ready, 1)

            def score(g, q, k, more=None):
                for t, (lo, hi) in enumerate(((0, P), (P, TW))):
                    last = pe.matmul(S[:, g, lo:hi], q(t), k(hi - lo), start=True, stop=more is None)
                    if more is not None:
                        last = pe.matmul(S[:, g, lo:hi], more[0](t), more[1](hi - lo), start=False, stop=True)
                return last

            def toks(x):
                return (lambda t: x[:, t * P:(t + 1) * P]), (lambda n: x[:, 0:n])

            def scores(kind, taken, gg=0, rot=None):
                pe.wait_ge(tile_taken, taken - 1)
                if kind == "dil":
                    for g in range(DG):
                        last = score(g, toks(qd[:, g])[0], toks(kd[:, g])[1])
                if kind == "nsa":
                    for g in range(2):
                        last = score(g, toks(qa[:])[0], toks(ksw[:, 2 * gg + g])[1])
                    for t in range(NT):
                        last = pe.matmul(S[:, 2, NCMP * t:NCMP * (t + 1)], qa[:, t * P:(t + 1) * P],
                                         kcmp[:, NCMP * gg:NCMP * (gg + 1)], start=True, stop=True)
                if kind == "mla":
                    base = slice(64 * rot, 64 * rot + 64)
                    last = score(0, toks(qm[:])[0], toks(km[:])[1],
                                 (toks(qpc[base])[0], toks(kpe[base])[1]))
                last.then_inc(scores_ready, 1)

            def transposes(kind, k, g, a=None):
                if a is not None:
                    pe.wait_ge(probs_ready, a + 1)
                if not isinstance(k, int) or k > 0:
                    pe.wait_ge(pt_taken, k)
                for c in range(3):
                    cols = slice(c * P, (c + 1) * P)
                    last = pe.transpose(PT[:, 0, cols], PROBS[kind][0][:, g, cols], ident[:])
                last.then_inc(pt_ready, 1)

            def cmp_transposes(k):
                for t in range(NT):
                    last = pe.transpose(S[0:NCMP, 2, P * (t + 1):P * (t + 2)], pcmp_s[:, t], ident[:])
                last.then_inc(pt_ready, 1)

            def weigh(kind, k, v0, v1, g, first, final):
                pe.wait_ge(pt_taken, k + 1)
                probsT = PROBS[kind][1]
                pe.matmul(O[:, 0, 0:SEQ], v0, probsT[:, g, 0:SEQ], start=first, stop=False)
                return pe.matmul(O[:, 0, P:SEQ], v1, probsT[:, g, SEQ:TW], start=False, stop=final)

            def slot_ops(j, a, kind, taken, g0, gg=0, rot=None):
                if j == 0:
                    if kind == "mla":
                        pe.wait_ge(qp_copied, rot[1])
                    scores(kind, taken, gg, None if rot is None else rot[0])
                if kind == "dil":
                    if j == 4:
                        if not isinstance(a, int) or a > 0:
                            pe.wait_ge(out_taken, a)
                        pe.wait_ge(v_copied, a + 1)
                    if 4 <= j <= 6:
                        g = j - 4
                        last = weigh(kind, g0 + g, v_cur[:, g, 0], v_cur[:, g, 1], g, g == 0, g == DG - 1)
                        if g == DG - 1:
                            last.then_inc(out_ready, 1)
                    if 3 <= j <= 5:
                        transposes(kind, g0 + j - 3, j - 3, a if j == 3 else None)
                if kind == "nsa":
                    if j == 2:
                        transposes(kind, g0, 0, a)
                        cmp_transposes(g0 + 1)
                    if j == 3:
                        transposes(kind, g0 + 2, 1)
                        pe.wait_ge(out_taken, a)
                        weigh(kind, g0, vt[:, 0, gg * P:(gg + 1) * P], vt[:, 1, gg * P:(gg + 1) * P], 0, True, False)
                        pe.matmul(O[:, 0, 0:SEQ], vcmp[:, gg], pcmpT[:], start=False, stop=False)
                        weigh(kind, g0 + 2, vt[:, 0, 256 + gg * P:256 + (gg + 1) * P],
                              vt[:, 1, 256 + gg * P:256 + (gg + 1) * P], 1, False, True).then_inc(out_ready, 1)
                if kind == "mla":
                    if j == 2:
                        transposes(kind, g0, 0, a)
                    if j == 3:
                        pe.wait_ge(out_taken, a)
                        pe.wait_ge(v_copied, a - (A_MLA - DH - 1))
                        weigh(kind, g0, v_head[:, 0], v_head[:, 1], 0, True, True).then_inc(out_ready, 1)

            pe.wait_ge(pool_set, 1)

            def h_ready(k):
                pe.wait_ge(h_lo, k + 1)

            def first_values():
                for k in range(KD):
                    h_ready(k)
                    b, n, s = 4 * k, k // 2, (k // 2) % R
                    if b % PB == 0:
                        pe.wait_ge(lo_split, n + 1)
                    half = slice((b % PB) * P, (b % PB + 4) * P)
                    for tt in range(NT):
                        tk = slice(tt * P, (tt + 1) * P)
                        out = proj[:, tt, :]
                        pe.matmul(out, hH[:, k, tk], wH[:, s, half], start=k == 0, stop=False)
                        pe.matmul(out, hL[:, k, tk], wH[:, s, half], start=False, stop=False)
                        last = pe.matmul(out, hH[:, k, tk], wL[:, s, half], start=False, stop=k == KD - 1)
                    if b % PB == 4:
                        last.then_inc(piece_used, 1)
                        start_up(k // 2)

            first_values()
            with pe.Fori(1, 4) as i:
                values(i * 2, 0, N_V, i, PB, hH, hL, KD)

            def dilated(d, attend):
                for t in range(8):
                    for half in range(2):
                        j = 2 * t + half
                        if attend:
                            slot_ops(j, d - 1, "dil", d * 8 + T_DIL, (d - 1) * DG)
                        if half == 0:
                            tile_free(d * 8 + (T_DIL + t))
                        tile_part(proj[:, t % 2, 0:SEQ], 16 * t + 8 * half, N_DIL, d, 16, hH, hL,
                                  range(8 * half, 8 * half + 8), half == 0, half == 1)

            dilated(0, False)
            with pe.Fori(1, DH) as d:
                dilated(d, True)

            for j in range(8):
                slot_ops(j, DH - 1, "dil", T_KSW, (DH - 1) * DG)
                t, half = j // 2, j % 2
                if half == 0:
                    tile_free(T_KSW + t)
                tile_part(proj[:, t % 2, 0:SEQ], 8 * j, N_KSW, 0, 0, hH, hL,
                          range(8 * half, 8 * half + 8), half == 0, half == 1)
                if j == 0:
                    pe.wait_ge(kcp_ready, 1)
                    pe.wait_ge(ms_taken, U_CMP)
                for m in (2 * j, 2 * j + 1):
                    w = m // 8
                    pe.wait_ge(w1_loaded[m % 2], 16 * (m // 2 + 1))
                    for b in range(PB):
                        s = (m % 8) * PB + b
                        last = pe.matmul(MS[:, 0, 8 * w:8 * w + 8], w1[:, m % 2, b * P:(b + 1) * P],
                                         kcp[:, w, s], start=s == 0, stop=s == NSA_BLOCK - 1)
                    last.then_inc(w1_used if m < 2 * NSA_BLOCK // PB - 1 else ms_ready, 1)

            def nsa(h, gg, attend):
                for t in range(2):
                    for half in range(2):
                        j = 2 * t + half
                        if attend:
                            slot_ops(j, h + (A_NSA - 1), "nsa", h * 2 + T_NSA, (h - 1) * 3 + G_NSA, gg)
                        if half == 0:
                            tile_free(h * 2 + (T_NSA + t))
                        tile_part(proj[:, t % 2, 0:SEQ], 16 * t + 8 * half, N_NSA, h, 4, hH, hL,
                                  range(8 * half, 8 * half + 8), half == 0, half == 1)
                        if not attend and j == 1:
                            pe.wait_ge(cs_ready, 1)
                            pe.wait_ge(ms_taken, U_CMP2)
                            pe.matmul(MS[:, 0, 0:8], w2[:, 0], cs[:, 0], start=True, stop=True)
                            for g in range(NSA_GROUPS):
                                last = pe.matmul(MS[0:NCMP, 0, P * (g + 1):P * (g + 2)],
                                                 cs[:, 1, NCMP * g:NCMP * (g + 1)], w2[:, 1], start=True, stop=True)
                            last.then_inc(ms_ready, 1)

            nsa(0, 0, False)
            pe.wait_ge(ms_taken, U_CMP2 + 1)
            for gg, (lo, hi) in enumerate(((1, NSA_HPG + 1), (NSA_HPG + 1, NSA_HEADS))):
                with pe.Fori(lo, hi) as h:
                    nsa(h, gg, True)

            def woe_outs(tile):
                return S[:, 1, 0:SEQ] if tile == 2 else proj[:, (T_WOE + tile) % 2, 0:SEQ]

            early = list(range(NSA_HEADS, EVEN_MIX)) + list(range(NSA_HEADS - 1))
            attn_at = {0: 0, 16: 2, 24: 3}
            b = 0
            for tile in range(3):
                for k, src in enumerate(early):
                    if b in attn_at:
                        slot_ops(attn_at[b], A_MLA - 1, "nsa", T_WOE, G_MLA - 3, NSA_GROUPS - 1)
                    if k == 0 and tile < 2:
                        tile_free(T_WOE + tile)
                    if b == 0:
                        pe.wait_ge(mix_lo, A_MLA - 1)
                    tile_part(woe_outs(tile), b, N_WOE, 0, 0, mixH, mixL, [src], k == 0, False)
                    b += 1
            pe.wait_ge(mix_lo, A_MLA)
            for tile in range(3):
                tile_part(woe_outs(tile), b, N_WOE, 0, 0, mixH, mixL, [NSA_HEADS - 1], False, True)
                b += 1
            for tile in range(3, KD):
                tile_free(T_WOE + tile)
                tile_part(woe_outs(tile), b, N_WOE, 0, 0, mixH, mixL, early + [NSA_HEADS - 1])
                b += EVEN_MIX

            def h2_ready(k):
                pe.wait_ge(h_lo, KD + k + 1)

            full(T_LAT, T_LAT, 0, N_LAT, 0, 0, hH, hL, KD, ready=h2_ready)
            norm_sums(U_NORM1, 1)
            full(T_LAT + 1, T_LAT + 1, KD, N_LAT, 0, 0, hH, hL, KD)
            with pe.Fori(1, KQ // 2) as i:
                for t in range(2):
                    full(i * 2 + (T_LAT + t), T_LAT + t, KD * t, N_LAT, i, 4, hH, hL, KD)
            for c in range(KKV + 1):
                full(T_LAT + KQ + c, T_LAT + KQ + c, KD * (KQ + c), N_LAT, 0, 0, hH, hL, KD)
                if c == 0:
                    norm_sums(U_NORMQ, 2)
            norm_sums(U_NORMKV, 3)

            b = 0
            for m in range(MH // 2):
                if m == 0:
                    pe.wait_ge(lat_lo, KQ)
                full(T_PE + m, T_PE + m, b, N_PE, 0, 0, latH, latL, KQ)
                b += KQ
            pe.wait_ge(lat_lo, KQ + KKV)
            kvH, kvL = latH[:, KQ:], latL[:, KQ:]
            for c in range(4):
                values(T_VM + 2 * c, 16 * c, N_VM, 0, 0, kvH, kvL, KKV, par=T_VM)

            def mla_pair(i, first):
                for bb in range(2):
                    t0 = T_MLA + 3 * bb
                    attend = not (first and bb == 0)
                    at = 32 * bb

                    def ops(j):
                        if attend:
                            slot_ops(j, i * 2 + (bb + A_MLA - 1), "mla", i * 6 + t0, i * 2 + (bb + G_MLA - 1),
                                     rot=(1 - bb, i + bb))

                    ops(0)
                    tile_free(i * 6 + t0)
                    tile_part(proj[:, t0 % 2, 0:SEQ], at, N_MLA, i, 8, latH, latL, range(KQ))
                    tile_free(i * 6 + (t0 + 1))
                    tile_part(proj[:, (t0 + 1) % 2, 0:SEQ], at + KQ, N_MLA, i, 8, kvH, kvL, range(KKV))
                    ops(2)
                    tile_free(i * 6 + (t0 + 2))
                    tile_part(proj[:, (t0 + 2) % 2, 0:SEQ], at + 16, N_MLA, i, 8, hH, hL, range(8), True, False)
                    ops(3)
                    tile_part(proj[:, (t0 + 2) % 2, 0:SEQ], at + 24, N_MLA, i, 8, hH, hL, range(8, 16), False, True)

            mla_pair(0, True)
            with pe.Fori(1, MH // 2) as i:
                mla_pair(i, False)

            b = 0
            for tile in range(2):
                for k in range(KD - 1):
                    if b in attn_at:
                        slot_ops(attn_at[b], A_MLA + MH - 1, "mla", T_WOO, G_MLA + MH - 1, rot=(1, MH // 2))
                    if k == 0:
                        tile_free(T_WOO + tile)
                    if b == 0:
                        pe.wait_ge(mix_lo, A_MLA + MH - 1)
                    tile_part(proj[:, (T_WOO + tile) % 2, 0:SEQ], b, N_WOO, 0, 0, mixH, mixL, [k], k == 0, False)
                    b += 1
            pe.wait_ge(mix_lo, A_MLA + MH)
            for tile in range(2):
                tile_part(proj[:, (T_WOO + tile) % 2, 0:SEQ], b, N_WOO, 0, 0, mixH, mixL, [KD - 1], False, True)
                b += 1
            with pe.Fori(1, KD // 2) as i:
                for t in range(2):
                    full(i * 2 + (T_WOO + t), T_WOO + t, KD * t, N_WOO, i, 4, mixH, mixL, KD)
            norm_sums(U_NORMF, 4)


def woe_end(tile):
    return 33 + tile if tile < 3 else EVEN_MIX * (tile + 1) - 1


def woe_mid(tile):
    return None if woe_end(tile) % PB == PB - 1 else [t for t in range(KD) if woe_end(t) % PB != PB - 1].index(tile)


def pe_tiles_ending(j):
    ends = [m for m in range(MH // 2) if (KQ * (m + 1) - 1) // PB == j]
    return (ends[0], ends[-1] + 1) if ends else (0, 0)


def _bucket(d):
    exact = BUCKETS // 2
    d = np.maximum(d, 0)
    big = exact + (np.log(np.maximum(d, 1).astype(np.float32) / exact) / math.log(MAX_DIST / exact)
                   * (BUCKETS - exact)).astype(np.int32)
    return np.where(d < exact, d, np.minimum(big, BUCKETS - 1))


def _constants():
    f = np.float32
    d = SEQ - 1 - np.arange(RRW)
    onehot = ((_bucket(d)[None, :] == np.arange(BUCKETS)[:, None]) & (d >= 0)[None, :]).astype(f)
    row_mask = np.zeros((HEADS_B, RRW), f)
    row_mask[:, d < 0] = NEG
    for g, (window, step) in enumerate(DIL):
        out = (d > window) | (d % step != 0) | (d < 0)
        row_mask[NSA_HEADS + g * DH:NSA_HEADS + (g + 1) * DH, out] = NEG
    t = np.arange(SEQ).reshape(NT, P)
    dist = t[:, None, :] - (np.arange(NCMP) * NSA_BLOCK + NSA_BLOCK - 1)[None, :, None]
    onehot_cmp = ((_bucket(dist)[None] == np.arange(BUCKETS)[:, None, None, None]) & (dist >= 0)[None])
    onehot_cmp = onehot_cmp.astype(f).reshape(BUCKETS, NT * NCMP, P)
    valid = (dist >= 0).transpose(2, 0, 1)
    cmp_mask = np.where(valid, 0.0, NEG).astype(f).reshape(P, NT * NCMP)
    tri = np.where(np.arange(P)[None, :] <= np.arange(P)[:, None], 0.0, NEG).astype(f)
    causal = np.concatenate([tri, np.zeros((P, P), f), tri], 1)
    half = ROPE // 2
    freqs = (1.0 / (f(10000.0) ** (np.arange(half, dtype=f) / f(half)))).astype(f)
    ang = freqs[:, None] * np.arange(SEQ, dtype=f)[None, :]
    cos, sin = np.cos(ang).astype(f), np.sin(ang).astype(f)
    cs = np.stack([np.tile(cos, (4, 1)), np.concatenate([-sin, sin, -sin, sin], 0)], 1)
    return dict(onehot=onehot, onehot_cmp=onehot_cmp, row_mask=row_mask, cmp_mask=cmp_mask,
                cmp_valid=valid.astype(f), causal=causal, rope_cs=cs, ident_in=np.eye(P, dtype=f))


def _stream(ev, evo, od, qb, kvb, odo):
    blocks = []

    def put(w, k, col):
        blocks.append(w[k * P:(k + 1) * P, col:col + P] if isinstance(col, int) else w[k * P:(k + 1) * P, col])

    q_a, kv_a, gate_a, qkv_b = 0, 1024, 2584, 3608
    gate_b = qkv_b + 3 * DG * DH * HD
    kc, vc, ks, vs, kw, vw = (kv_a + 256 * n for n in range(6))
    vb = qkv_b + 2 * DG * DH * HD
    chunks = [[vs, vs + P, vw, vw + P]] + [[vb + (g * DH + d) * P for d in range(DH)] for g in range(DG)]
    for cols in chunks:
        for k in range(KD):
            for c in cols:
                put(ev, k, c)
    for d in range(DH):
        cols = [qkv_b + (g * DH + d) * P for g in range(DG)]
        cols += [qkv_b + (DG * DH + g * DH + d) * P for g in range(DG)]
        cols += [(kc, kc + P, vc, vc + P)[d], gate_b + d * P]
        for c in cols:
            for k in range(KD):
                put(ev, k, c)
    for c in (ks, kw, ks + P, kw + P):
        for k in range(KD):
            put(ev, k, c)
    for h in range(NSA_HEADS):
        for c in (q_a + h * P, gate_a + h * P):
            for k in range(KD):
                put(ev, k, c)
    early = list(range(NSA_HEADS, EVEN_MIX)) + list(range(NSA_HEADS - 1))
    for tile in range(3):
        for k in early:
            put(evo, k, tile * P)
    for tile in range(3):
        put(evo, NSA_HEADS - 1, tile * P)
    for tile in range(3, KD):
        for k in early + [NSA_HEADS - 1]:
            put(evo, k, tile * P)
    for c in range(KQ + KKV):
        for k in range(KD):
            put(od, k, c * P)
    twice = np.tile(np.arange(QR + KVR, QR + KVR + ROPE), 2)
    for k in range(KD):
        put(od, k, twice)
    hq, hkv = NOPE + ROPE, NOPE + MV
    for m in range(MH // 2):
        cols = np.concatenate([np.arange(ROPE) + (2 * m + b) * hq + NOPE for b in range(2)])
        for k in range(KQ):
            put(qb, k, cols)
    for c in range(4):
        for k in range(KKV):
            for h in range(4 * c, 4 * c + 4):
                put(kvb, k, h * hkv + NOPE)
    for h in range(MH):
        for k in range(KQ):
            put(qb, k, h * hq)
        for k in range(KKV):
            put(kvb, k, h * hkv)
        for k in range(KD):
            put(od, k, QR + KVR + ROPE + h * P)
    for tile in range(2):
        for k in range(KD - 1):
            put(odo, k, tile * P)
    for tile in range(2):
        put(odo, KD - 1, tile * P)
    for tile in range(2, KD):
        for k in range(KD):
            put(odo, k, tile * P)
    assert len(blocks) == N_END * PB
    out = np.empty((N_END, P, PB, P), np.float32)
    for n, b in enumerate(blocks):
        out[n // PB, :, n % PB] = b
    return out.reshape(N_END, P, PW)


def kernel(x, rel_bias, norm_w, final_norm_w, ev_w_in, nsa_cmp_pos, nsa_cmp_w1, nsa_cmp_w2,
           ev_w_out, od_w_in, mla_q_norm, mla_w_qb, mla_kv_norm, mla_w_kvb, od_w_out):
    import concourse.bacc as bacc
    from concourse.bass_utils import run_bass_kernel_spmd

    a = {k: np.asarray(v) for k, v in dict(
        x=x, ev=ev_w_in, evo=ev_w_out, od=od_w_in, qb=mla_w_qb, kvb=mla_w_kvb, odo=od_w_out,
        w1=nsa_cmp_w1, w2=nsa_cmp_w2, pos=nsa_cmp_pos, tab=rel_bias, nw=norm_w, fw=final_norm_w,
        qn=mla_q_norm, kvn=mla_kv_norm).items()}
    arrays = dict(
        x_in=a["x"][0].T.reshape(KD, P, SEQ).transpose(1, 0, 2),
        w_stream=_stream(a["ev"][0], a["evo"][0], a["od"][0], a["qb"][0], a["kvb"][0], a["odo"][0]),
        w_gate3=a["ev"][0][:, 2560:2584].reshape(KD, P, 24).transpose(1, 0, 2),
        w_cmp1=a["w1"][0].reshape(2 * NSA_BLOCK // PB, PB, P, P).transpose(0, 2, 1, 3).reshape(-1, P, PW),
        w_cmp2=a["w2"][0].transpose(1, 0, 2),
        cmp_pos=a["pos"][0].transpose(2, 0, 1),
        table=a["tab"],
        norms=np.concatenate([a["nw"], a["fw"][None]], 0).reshape(3, KD, P).transpose(2, 0, 1),
        q_norm=a["qn"][0].reshape(KQ, P).T,
        kv_norm=a["kvn"][0].reshape(KKV, P).T,
        **_constants())
    nc = bacc.Bacc("TRN2", target_bir_lowering=False, num_devices=1)
    args, feeds = {}, {}
    for name, v in arrays.items():
        v = np.ascontiguousarray(v)
        feeds[name + "_dram"] = v
        args[name] = nc.dram_tensor(name + "_dram", v.shape, mybir.dt.from_np(v.dtype), kind="ExternalInput").ap()
    y = nc.dram_tensor("y_dram", (P, KD, SEQ), mybir.dt.float32, kind="ExternalOutput").ap()
    trunk(nc, y_out=y, **args)
    r = run_bass_kernel_spmd(nc, [feeds], core_ids=[0])
    got = r.results[0]["y_dram"]
    return got.transpose(2, 1, 0).reshape(1, SEQ, D_MODEL)
```

```python
import math
from contextlib import ExitStack

import numpy as np
import concourse.bass as bass
from concourse import mybir

P = 128
D_MODEL, SEQ, HD = 2048, 256, 128
EPS, NEG = 1e-6, -1e30
NT = SEQ // P
KD = D_MODEL // P
BUCKETS, MAX_DIST = 32, 2048
NSA_HEADS, NSA_GROUPS, NSA_BLOCK = 8, 2, 64
NSA_HPG = NSA_HEADS // NSA_GROUPS
NCMP = SEQ // NSA_BLOCK
DIL = ((128, 1), (512, 4), (2048, 16))
DG, DH = 3, 4
HEADS_B = NSA_HEADS + DG * DH
MH, QR, KVR, NOPE, ROPE, MV = 16, 1536, 512, 128, 64, 128
KQ, KKV = QR // P, KVR // P
EVEN_MIX = NSA_HEADS + DH
PB = 8
PW = PB * P
R = 4
XR = 4
LEAD = R - 1
TW = 3 * P
RRW = 3 * P

N_V, N_DIL = 0, NT * 2 * PB
N_KSW = N_DIL + DH * 16
KSW_ORDER = "k" + "kww" * 7 + "ww"
N_NSA = N_KSW + len(KSW_ORDER)
N_WOE = N_NSA + NSA_HEADS * 4
N_LAT = N_WOE + KD * EVEN_MIX // PB
N_PE = N_LAT + 2 * (KQ + KKV + 1)
N_VM = N_PE + (MH // 2) * KQ // PB
N_MLA = N_VM + 8
N_WOO = N_MLA + MH * 4
N_END = N_WOO + 2 * KD
T_DIL = 8
T_KSW = T_DIL + DH * 8
T_NSA = T_KSW + 4
T_WOE = T_NSA + NSA_HEADS * 2
T_LAT = T_WOE + KD
T_PE = T_LAT + KQ + KKV + 1
T_VM = T_PE + MH // 2
T_MLA = T_VM + 8
T_WOO = T_MLA + MH * 3
MID_WOE, MID_PE = 0, 9
MID_MLA = MID_PE + MH // 4
MID_WOO = MID_MLA + MH
CONSTS_B = 8
WARM = 20
BIAS_SETS = DH + NSA_HEADS // 2
A_NSA = DH
A_MLA = A_NSA + NSA_HEADS
G_NSA = DH * DG
G_MLA = G_NSA + NSA_HEADS * 3
U_BIAS, U_CBIAS, U_NORM0, U_GATE3, U_GATE3T, U_CMP, U_CMPS, U_CMP2, U_NORM1, U_NORMQ, U_NORMKV, U_NORMF = \
    range(12)
DVE_OUT, POOL_OUT = range(0, 6), range(6, 8)
VM_BANKS = (2, 0, 4, 2)
DVE_TURN = {"dil": 4, "nsa": 6, "lat": 4, "mla": 6, "woo": 8}


def ms_count(use):
    return use + 1 - (use > U_CMP)


class Tally:

    def __init__(self, eng, sem):
        self.eng, self.sem, self.base, self.n = eng, sem, 0, 0

    def link(self, ins):
        ins.then_inc(self.sem, 1)
        self.n += 1
        self.eng.wait_ge(self.sem, self.base + self.n)

    def turn(self, i, per_turn):
        self.entry, self.per = self.base + self.n, per_turn
        self.base, self.n = self.entry + i * per_turn, 0

    def leave(self, turns):
        assert self.n == self.per, (self.n, self.per)
        self.base, self.n = self.entry + turns * self.per, 0


def trunk(nc, x_in, w_stream, w_gate3, w_cmp2, cmp_pos, table, norms, q_norm, kv_norm,
          onehot, onehot_cmp, row_mask, cmp_mask, cmp_valid, causal, rope_cs, ident_in, sel_in, y_out):
    f32, f32r = mybir.dt.float32, mybir.dt.float32r
    ALU, ACT, AX = mybir.AluOpType, mybir.ActivationFunctionType, mybir.AxisListType
    MUL, ADD, SUB, MAX = ALU.mult, ALU.add, ALU.subtract, ALU.max
    ROOT = math.sqrt(HD)
    SC_EVEN, SC_MLA = HD ** -0.5, (NOPE + ROPE) ** -0.5
    ds = bass.ds

    x_mid = nc.dram_tensor("x_mid", (P, KD, SEQ), f32)
    bias_rows = nc.dram_tensor("bias_rows", (HEADS_B, P, RRW), f32)

    ctx = ExitStack()
    with ctx:
        def sb(name, shape, dt=f32, into=ctx):
            return into.enter_context(nc.sbuf_tensor(name, shape, dt))

        def sem(name):
            return ctx.enter_context(nc.semaphore(name))

        hH, hL = sb("hH", [P, KD, SEQ], f32r), sb("hL", [P, KD, SEQ], f32r)
        raw = sb("raw", [P, R, PW])
        w_hl = sb("w_hl", [P, 2, R, PW], f32r)
        wH, wL = w_hl[:, 0], w_hl[:, 1]
        vt = sb("vt", [P, NT, D_MODEL])
        xr = sb("xr", [P, XR, SEQ])
        rfac = sb("rfac", [P, SEQ + NT])
        rq = sb("rq", [P, SEQ + NT])
        rkv = sb("rkv", [P, SEQ + NT])
        rtmp, rvar, rnew = sb("rtmp", [P, NT]), sb("rvar", [P, NT]), sb("rnew", [P, NT])
        diag = sb("diag", [P, NT, P])
        gate_z, gate_t, gate_g = sb("gate_z", [P, SEQ]), sb("gate_t", [P, SEQ]), sb("gate_g", [P, SEQ])
        mixf = sb("mixf", [P, SEQ])
        mx, nmx = sb("mx", [P, NT, DG]), sb("nmx", [P, NT, DG])
        den, coef = sb("den", [P, NT, DG]), sb("coef", [P, NT, DG])
        mx1, tick, tick_p = sb("mx1", [P, NT]), sb("tick", [P, 16]), sb("tick_p", [P, 1])
        ident, ones = sb("ident", [P, P]), sb("ones", [P, P])
        nrm = sb("nrm", [P, 3, KD])
        qn, kvn = sb("qn", [P, KQ]), sb("kvn", [P, KKV])
        zt, zw = sb("zt", [P, 2, SEQ]), sb("zw", [P, 2, SEQ])
        zs = sb("zs", [P, SEQ])
        sq, acc = sb("sq", [P, 2, SEQ]), sb("acc", [P, SEQ])
        nrm_sum = sb("nrm_sum", [P, SEQ])

        csum = zt[0:16].rearrange("p w (a e) -> p w a e", a=2)
        sel = sb("sel", [16, 8])

        start = ExitStack()
        xT = sb("xT", [P, KD, SEQ], into=start)
        sq0 = sb("sq0", [P, 2, 4, SEQ], into=start)
        sq4 = sb("sq4", [P, 4, SEQ], into=start)
        oneh = sb("oneh", [BUCKETS, RRW], into=start)
        oneh_c = sb("oneh_c", [BUCKETS, NT * NCMP, P], into=start)
        start.close()
        mixH, mixL = sb("mixH", [P, KD, SEQ], f32r), sb("mixL", [P, KD, SEQ], f32r)

        even = ExitStack()
        qd, kd = sb("qd", [P, DG, SEQ], into=even), sb("kd", [P, DG, SEQ], into=even)
        probs_e = sb("probs_e", [P, DG, TW], into=even)
        probsT_e = sb("probsT_e", [P, DG, TW], into=even)
        v_cur = sb("v_cur", [P, DG, NT, P], into=even)
        kvc = sb("kvc", [P, 4, SEQ], into=even)
        ksw = sb("ksw", [P, 4, SEQ], into=even)
        qa = sb("qa", [P, SEQ], into=even)
        kcp = sb("kcp", [P, 2, NSA_BLOCK, NSA_GROUPS * NCMP], into=even)
        kcHL = sb("kcHL", [P, 2, NSA_BLOCK, 16], f32r, even)
        w2 = sb("w2", [P, 2, P], into=even)
        posT = sb("posT", [P, 2, NSA_BLOCK], into=even)
        cz, ct, cs = [sb(n, [P, 2, 8], into=even) for n in ("cz", "ct", "cs")]
        kcmp = sb("kcmp", [P, 8], into=even)
        vcmp = sb("vcmp", [NCMP, NSA_GROUPS, P], into=even)
        bias = sb("bias", [P, DG, SEQ], into=even)
        cbias = sb("cbias", [P, NSA_HEADS, NT * NCMP], into=even)
        cmask = sb("cmask", [P, NT * NCMP], into=even)
        cvalid = sb("cvalid", [P, NT, NCMP], into=even)
        pcmp, pcmp_s = sb("pcmp", [P, NT, NCMP], into=even), sb("pcmp_s", [P, NT, NCMP], into=even)
        pcmpT = sb("pcmpT", [NCMP, SEQ], into=even)
        tab = sb("tab", [BUCKETS, HEADS_B], into=even)
        rmask, rows = sb("rmask", [HEADS_B, RRW], into=even), sb("rows", [HEADS_B, RRW], into=even)
        g3w = sb("g3w", [P, KD, 24], into=even)
        g3H, g3L = sb("g3H", [P, KD, 24], f32r, even), sb("g3L", [P, KD, 24], f32r, even)
        g3c = zs[0:24]
        g3z, g3t = sb("g3z", [P, NT, 24], into=even), sb("g3t", [P, NT, 24], into=even)
        g3s = sb("g3s", [P, NSA_HEADS, NT, 3], into=even)
        even.close()
        odd = ExitStack()
        latH = sb("latH", [P, KQ + KKV, SEQ], f32r, odd)
        latL = sb("latL", [P, KQ + KKV, SEQ], f32r, odd)
        probs_o = sb("probs_o", [P, 1, TW], into=odd)
        probsT_o = sb("probsT_o", [P, 1, TW], into=odd)
        v_head = sb("v_head", [P, NT, P], into=odd)
        qpe, kpe = sb("qpe", [P, MH // 2, SEQ], into=odd), sb("kpe", [P, SEQ], into=odd)
        qpc, qm, km = [sb(n, [P, SEQ], into=odd) for n in ("qpc", "qm", "km")]
        rt1, rt2 = sb("rt1", [P, SEQ], into=odd), sb("rt2", [P, SEQ], into=odd)
        cossin, cmask_m = sb("cossin", [P, 2, SEQ], into=odd), sb("cmask_m", [P, TW], into=odd)
        odd.close()
        yw = sb("yw", [P, KD, SEQ])
        PROBS = {"dil": (probs_e, probsT_e), "nsa": (probs_e, probsT_e), "mla": (probs_o, probsT_o)}

        banks = ctx.enter_context(nc.psum_tensor("banks", [P, 8, 512], f32))
        proj, S, PT, O, MS = (banks[:, lo:hi] for lo, hi in ((0, 2), (2, 5), (5, 6), (6, 7), (7, 8)))

        loaded = [sem(f"piece_loaded{s}") for s in range(R)]
        x_loaded = [sem(f"x_loaded{c}") for c in range(KD // 2)]
        consts_bias = sem("consts_bias")
        consts_a, consts_b, consts_odd = sem("consts_early"), sem("consts_late"), sem("consts_odd")
        rows_ready = sem("rows_ready")
        rows_stored, bias_loaded = sem("rows_stored"), sem("bias_loaded")
        stored, x_stored = sem("stored"), sem("x_stored")
        xr_loaded = [sem(f"xr_loaded{c}") for c in range(XR)]
        xm_loaded = [sem(f"xm_loaded{c}") for c in range(XR)]
        hi_split, lo_split, piece_used = sem("hi_split"), sem("lo_split"), sem("piece_used")
        mid_tile, tile_taken = sem("mid_tile"), sem("tile_taken")
        h_hi, h_lo, g3_hi, g3_lo = sem("h_hi"), sem("h_lo"), sem("g3_hi"), sem("g3_lo")
        x_new, lat_z, lat_hi, lat_lo = sem("x_new"), sem("lat_z"), sem("lat_hi"), sem("lat_lo")
        ms_ready, ms_taken = sem("ms_ready"), sem("ms_taken")
        inv_ready, rfac_ready = sem("inv_ready"), sem("rfac_ready")
        squares, squares_used, acc_ready = sem("squares"), sem("squares_used"), sem("acc_ready")
        last_square, diag_ready, spread_ready = sem("last_square"), sem("diag_ready"), sem("spread_ready")
        scores_ready, logits_ready = sem("scores_ready"), sem("logits_ready")
        exp_ready, probs_ready = sem("exp_ready"), sem("probs_ready")
        pt_ready, pt_taken = sem("pt_ready"), sem("pt_taken")
        out_ready, out_taken = sem("out_ready"), sem("out_taken")
        mix_hi, mix_lo = sem("mix_hi"), sem("mix_lo")
        gz_ready, gt_ready = sem("gz_ready"), sem("gt_ready")
        v_copied, qp_copied = sem("v_copied"), sem("qp_copied")
        kc_hi, kc_lo, csum_ready = sem("kc_hi"), sem("kc_lo"), sem("csum_ready")
        kcp_ready, cz_ready, ct_ready, cs_ready = sem("kcp_ready"), sem("cz_ready"), sem("ct_ready"), sem("cs_ready")
        g3z_ready, g3t_ready, g3c_ready = sem("g3z_ready"), sem("g3t_ready"), sem("g3c_ready")
        rope_z, rope_s, rotated = sem("rope_z"), sem("rope_s"), sem("rotated")
        pool_set, pool_chain, dve_chain = sem("pool_set"), sem("pool_chain"), sem("dve_chain")
        factor_copied = sem("factor_copied")
        y_ready, y_ready_p, stored_p = sem("y_ready"), sem("y_ready_p"), sem("stored_p")

        block = ctx.enter_context(nc.Block())

        def scale_out(eng, c, factor):
            xc = yw[:, 2 * c:2 * c + 2, :]
            fac = factor.rearrange("p (a n) -> p a n", a=1).to_broadcast([P, 2, SEQ])
            return eng.tensor_tensor(xc, xc, fac, MUL)

        @block.sync
        def _(sp):
            sp.dma_start(nrm[:], norms).then_inc(consts_a, 16)
            for c in range(KD // 2):
                sp.dma_start(xT[:, 2 * c:2 * c + 2, :], x_in[:, 2 * c:2 * c + 2, :]).then_inc(x_loaded[c], 16)
                if c < R:
                    sp.dma_start(raw[:, c, :], w_stream[c]).then_inc(loaded[c], 16)
                if c == 2:
                    for dst, src in ((tab, table), (oneh, onehot), (oneh_c, onehot_cmp), (rmask, row_mask),
                                     (cmask, cmp_mask)):
                        sp.dma_start(dst[:], src).then_inc(consts_bias, 16)
            for dst, src in ((cvalid, cmp_valid), (g3w, w_gate3), (ident, ident_in), (posT, cmp_pos),
                             (w2, w_cmp2), (qn, q_norm), (kvn, kv_norm), (sel, sel_in)):
                sp.dma_start(dst[:], src).then_inc(consts_b, 16)
            for s in range(R):
                sp.wait_ge(lo_split, s + 1)
                sp.dma_start(raw[:, s, :], w_stream[R + s]).then_inc(loaded[s], 16)
            last = N_END // R
            with sp.Fori(2, last) as i:
                for s in range(R):
                    sp.wait_ge(lo_split, i * R + (s - R + 1))
                    sp.dma_start(raw[:, s, :],
                                 w_stream[ds(i * R + s, 1)].rearrange("a p n -> p (a n)")).then_inc(loaded[s], 16)
            for s in range(N_END % R):
                sp.wait_ge(lo_split, last * R + s - R + 1)
                sp.dma_start(raw[:, s, :], w_stream[last * R + s]).then_inc(loaded[s], 16)
            for c in DVE_OUT:
                sp.wait_ge(y_ready, c + 1)
                sp.dma_start(y_out[:, 2 * c:2 * c + 2, :], yw[:, 2 * c:2 * c + 2, :]).then_inc(stored, 16)
            sp.wait_ge(stored, 16 * len(DVE_OUT))

        @block.gpsimd
        def _(pool):
            chain = Tally(pool, pool_chain)
            pool.memset(ones[:], 1.0).then_inc(pool_set, 1)
            for c in range(4):
                pool.wait_ge(x_loaded[2 * c], 16)
                pool.wait_ge(x_loaded[2 * c + 1], 16)
                if c >= 2:
                    pool.wait_ge(squares_used, c - 1)
                xc = xT[:, 4 * c:4 * c + 4, :]
                pool.tensor_tensor(sq0[:, c % 2], xc, xc, MUL).then_inc(squares, 1)

            pool.wait_ge(rows_ready, 1)
            for k in range(BIAS_SETS):
                pool.wait_ge(piece_used, 6 + 3 * k)
                if k > 0:
                    pool.wait_ge(rows_stored, 16 * k)
                heads = slice(NSA_HEADS + k, HEADS_B, DH) if k < DH else slice(2 * (k - DH), 2 * (k - DH) + 2)
                src = rows[heads].rearrange("h (a n) -> h a n", a=1)
                pool.dma_start(bias_rows.ap()[heads], src.to_broadcast([src.shape[0], P, RRW])).then_inc(rows_stored, 16)

            def copy_v_dilated(d):
                pool.wait_ge(tile_taken, T_DIL)
                for g in range(DG):
                    src = vt[:, :, ds(d * P + 512 * (g + 1), P)]
                    c = pool.tensor_copy(v_cur[:, g], src)
                c.then_inc(v_copied, 1)

            copy_v_dilated(0)
            with pool.Fori(1, DH) as d:
                pool.wait_ge(out_ready, d)
                copy_v_dilated(d)

            def add_square(k, src, first, out=acc):
                chain.link(pool.tensor_tensor(sq[:, k % 2], src, src, MUL))
                if first:
                    return pool.tensor_copy(acc[:], sq[:, k % 2])
                return pool.tensor_tensor(out[:], acc[:], sq[:, k % 2], ADD)

            for c in range(KD):
                pool.wait_ge(x_new, c + 1)
                if c < KD - 2:
                    chain.link(add_square(c, xr[:, c % XR], c == 0))
                elif c == KD - 2:
                    add_square(c, xr[:, c % XR], False, nrm_sum).then_inc(acc_ready, 1)
                    pool.wait_ge(acc_ready, 1)
                if c > 0:
                    pool.wait_ge(x_stored, 16 * c)
                pool.dma_start(x_mid.ap()[:, c], xr[:, c % XR]).then_inc(x_stored, 16)
            pool.wait_ge(x_stored, 16 * KD)
            pool.wait_ge(h_lo, 2 * KD)
            pool.wait_ge(last_square, 1)
            for c in range(XR):
                pool.dma_start(xr[:, c], x_mid.ap()[:, c]).then_inc(xm_loaded[c], 16)
            pool.dma_start(cossin[:], rope_cs).then_inc(consts_odd, 16)
            pool.dma_start(cmask_m[:], causal).then_inc(consts_odd, 16)
            for lo, hi in ((0, KQ), (KQ, KQ + KKV)):
                for c in range(lo, hi - 1):
                    pool.wait_ge(lat_z, c + 1)
                    if c == lo:
                        pool.wait_ge(ms_taken, U_NORM1 + 1 if lo == 0 else U_NORMQ + 1)
                    add_square(c, zt[:, c % 2], c == lo, acc if c < hi - 2 else nrm_sum).then_inc(squares, 1)
                    if c < hi - 2:
                        pool.wait_ge(squares, 4 + c + (lo == 0))
                    else:
                        pool.wait_ge(squares, 4 + c + (lo == 0))
                        pool.memset(tick_p[:, 0:1], 0.0).then_inc(acc_ready, 1)

            pool.wait_ge(consts_odd, 32)
            for k in range(1, 2 + MH // 2):
                if k > 1:
                    pool.wait_ge(rotated, k - 1)
                pool.wait_ge(rope_z, k)
                pool.tensor_tensor(rt1[:], zt[:, (k - 1) % 2], cossin[:, 0], MUL)
                pool.wait_ge(rope_s, k)
                chain.link(pool.tensor_tensor(rt2[:], zs[:], cossin[:, 1], MUL))
                out = kpe[:] if k == 1 else qpe[:, k - 2]
                pool.tensor_tensor(out, rt1[:], rt2[:], ADD).then_inc(rotated, 1)
            pool.wait_ge(rotated, 1 + MH // 2)

            def copy_v_mla(h):
                pool.tensor_copy(v_head[:], vt[:, :, ds(h * MV, MV)]).then_inc(v_copied, 1)

            def copy_qpe(i):
                pool.tensor_copy(qpc[:], qpe[:, ds(i, 1), :].rearrange("p a n -> p (a n)")).then_inc(qp_copied, 1)

            with pool.Fori(0, MH // 2) as i:
                pool.wait_ge(scores_ready, i * 2 + A_MLA)
                pool.wait_ge(tile_taken, T_MLA)
                copy_qpe(i)
                for b in range(2):
                    pool.wait_ge(out_ready, i * 2 + b + A_MLA)
                    pool.wait_ge(tile_taken, T_MLA)
                    copy_v_mla(i * 2 + b)
            for c in range(KD - 1):
                pool.wait_ge(x_new, KD + c + 1)
                if c == 0:
                    pool.wait_ge(ms_taken, U_NORMKV + 1)
                add_square(c, zt[:, c % 2], c == 0, acc if c < KD - 2 else nrm_sum).then_inc(squares, 1)
                pool.wait_ge(squares, 2 + KQ + KKV + c + 1)
                if c + XR < KD:
                    pool.dma_start(xr[:, c % XR], x_mid.ap()[:, c + XR]).then_inc(xm_loaded[c % XR], 16)
            pool.memset(tick_p[:, 0:1], 0.0).then_inc(acc_ready, 1)
            pool.wait_ge(factor_copied, 1)
            for c in POOL_OUT:
                scale_out(pool, c, rfac[:, 0:SEQ]).then_inc(y_ready_p, 1)

        @block.scalar
        def _(act):
            def split(n, s, count):
                act.wait_ge(loaded[s], count * 16)
                if not isinstance(n, int) or n >= R:
                    act.wait_ge(piece_used, n - (R - 1))
                act.activation(wH[:, s], raw[:, s], ACT.Copy).then_inc(hi_split, 1)

            def split_at(n):
                if n < N_END:
                    split(n, n % R, n // R + 1)

            def split_in(n0, i, per, j):
                m = n0 + j
                split(i * per + m, m % R, i * (per // R) + (m // R + 1))

            def gate_tanh(a):
                act.wait_ge(gz_ready, a + 1)
                act.activation(gate_t[:], gate_z[:], ACT.Tanh, scale=0.5).then_inc(gt_ready, 1)

            def exps(a, kind):
                act.wait_ge(logits_ready, a + 1)
                probs = PROBS[kind][0]
                if kind == "dil":
                    for t in range(NT):
                        v = probs[:, :, 0:P] if t == 0 else probs[:, :, P:TW]
                        e = act.activation(v, v, ACT.Exp, bias=nmx[:, t, 0:1], scale=SC_EVEN,
                                           accum_out=den[:, t, 0:1])
                if kind == "nsa":
                    act.activation(pcmp[:], pcmp[:], ACT.Exp, scale=SC_EVEN)
                if kind in ("nsa", "mla"):
                    for g in range(2 if kind == "nsa" else 1):
                        for t in range(NT):
                            v = probs[:, g, 0:P] if t == 0 else probs[:, g, P:TW]
                            col = g + 1 if kind == "nsa" else 0
                            e = act.activation(v, v, ACT.Exp, bias=nmx[:, t, col:col + 1],
                                               scale=SC_EVEN if kind == "nsa" else SC_MLA,
                                               accum_out=den[:, t, col:col + 1])
                e.then_inc(exp_ready, 1)

            def take_pt(k, g, kind):
                act.wait_ge(pt_ready, k + 1)
                if kind == "cmp":
                    act.activation(pcmpT[:], S[0:NCMP, 2, P:P + SEQ], ACT.Copy).then_inc(pt_taken, 1)
                else:
                    src = S[:, 0, 0:TW] if kind == "nsa" and g == 1 else PT[:, 0, 0:TW]
                    act.activation(PROBS[kind][1][:, g], src, ACT.Copy).then_inc(pt_taken, 1)

            def mix_high(a, idx):
                act.wait_ge(out_taken, a + 1)
                out = mixH[:, idx] if isinstance(idx, int) else mixH[:, ds(idx, 1), :].rearrange("p a n -> p (a n)")
                act.activation(out, mixf[:], ACT.Copy).then_inc(mix_hi, 1)

            def load_bias(a, row0, step, n):
                if not isinstance(a, int) or a > 0:
                    act.wait_ge(logits_ready, a)
                act.wait_ge(rows_stored, 16 * BIAS_SETS if n == 1 else a * 16 + 16)
                for g in range(n):
                    r = row0 + g * step
                    src = bass.AP(bias_rows, r * (P * RRW) + (P - 1), [[RRW - 1, P], [1, SEQ]])
                    act.dma_start(bias[:, g, :], src).then_inc(bias_loaded, 16)

            def slot_ops(j, a, idx, kind, g0):
                if j == 0:
                    gate_tanh(a)
                    exps(a, kind)
                    if kind == "dil" and isinstance(a, int) and a == DH - 1:
                        load_bias(A_NSA, 0, 0, 1)
                if kind == "dil":
                    if 3 <= j <= 5:
                        take_pt(g0 + j - 3, j - 3, kind)
                    if j == 6:
                        mix_high(a, idx)
                if kind == "nsa":
                    if j == 2:
                        take_pt(g0, 0, kind)
                        take_pt(g0 + 1, 0, "cmp")
                        take_pt(g0 + 2, 1, kind)
                    if j == 3:
                        mix_high(a, idx)
                if kind == "mla":
                    if j == 2:
                        take_pt(g0, 0, kind)
                    if j == 3:
                        mix_high(a, idx)

            act.wait_ge(consts_a, 16)
            for c in range(KD):
                act.wait_ge(x_loaded[c // 2], 16)
                act.activation(hH[:, c], xT[:, c], ACT.Copy, scale=nrm[:, 0, c:c + 1]).then_inc(h_hi, 1)
                if c % 2 and c // 2 < R:
                    split_at(c // 2)
            act.wait_ge(consts_b, 16 * CONSTS_B)
            act.activation(g3H[:], g3w[:], ACT.Copy).then_inc(g3_hi, 1)
            for j in range(PB):
                if j + LEAD >= R:
                    split_at(j + LEAD)
                if j == 5:
                    act.wait_ge(inv_ready, 1)
                    act.activation(rfac[:, SEQ:], rtmp[:], ACT.Sqrt).then_inc(rfac_ready, 1)
            with act.Fori(1, 4) as i:
                for j in range(PB):
                    split_in(N_V, i, PB, j + LEAD)
            for j in range(16):
                split_at(N_DIL + j + LEAD)
                if j == 0:
                    load_bias(0, NSA_HEADS, DH, DG)
                    act.wait_ge(g3z_ready, 1)
                    act.activation(g3t[:], g3z[:], ACT.Tanh, scale=0.5).then_inc(g3t_ready, 1)
            with act.Fori(1, DH) as d:
                for j in range(16):
                    split_in(N_DIL, d, 16, j + LEAD)
                    slot_ops(j, d - 1, d + (NSA_HEADS - 1), "dil", (d - 1) * DG)
                    if j == 0:
                        load_bias(d, d + NSA_HEADS, DH, DG)
            j = 0
            for p, kind in enumerate(KSW_ORDER):
                if p == 0:
                    act.wait_ge(kcp_ready, 1)
                    act.activation(kcHL[:, :, :, 0:8], kcp[:], ACT.Copy).then_inc(kc_hi, 1)
                split_at(N_KSW + p + LEAD)
                if kind == "k":
                    slot_ops(j, DH - 1, NSA_HEADS + DH - 1, "dil", (DH - 1) * DG)
                    j += 1
            act.wait_ge(cz_ready, 1)
            act.activation(ct[:], cz[:], ACT.Tanh, scale=0.5).then_inc(ct_ready, 1)
            for j in range(4):
                split_at(N_NSA + j + LEAD)
            with act.Fori(1, NSA_HEADS) as h:
                for j in range(4):
                    split_in(N_NSA, h, 4, j + LEAD)
                    slot_ops(j, h + (A_NSA - 1), h - 1, "nsa", (h - 1) * 3 + G_NSA)
                    if j == 0:
                        load_bias(h + A_NSA, h, 0, 1)
            for c in range(XR):
                act.dma_start(xr[:, c], x_in[:, c]).then_inc(xr_loaded[c], 16)
            tile = 0
            for j in range(KD * EVEN_MIX // PB):
                split_at(N_WOE + j + LEAD)
                if j < 4:
                    slot_ops(j, A_MLA - 1, NSA_HEADS - 1, "nsa", G_MLA - 3)
                while tile < KD and woe_end(tile) < (j + 1) * PB:
                    act.wait_ge(x_new, tile + 1)
                    act.activation(hH[:, tile], xr[:, tile % XR], ACT.Copy,
                                   scale=nrm[:, 1, tile:tile + 1]).then_inc(h_hi, 1)
                    if XR - 1 <= tile < KD - XR + 2:
                        act.wait_ge(x_stored, 16 * (tile - 1))
                        act.wait_ge(h_lo, KD + tile - 1)
                        act.wait_ge(pool_chain, 2 * (tile - 1))
                        for c in range(XR if tile == XR - 1 else tile + XR - 2, tile + XR - 1):
                            act.dma_start(xr[:, c % XR], x_in[:, c]).then_inc(xr_loaded[c % XR], 16)
                    tile += 1

            def square_last(src):
                act.activation(zs[:], src, ACT.Square).then_inc(last_square, 1)

            square_last(xr[:, (KD - 1) % XR])

            def latent_high(c):
                act.wait_ge(lat_z, c + 1)
                out = latH[:, c] if isinstance(c, int) else latH[:, ds(c, 1), :].rearrange("p a n -> p (a n)")
                return out

            def latent_pair(n0, i, c0):
                for j in range(4):
                    if isinstance(i, int):
                        split_at(n0 + i * 4 + j + LEAD)
                    else:
                        split_in(n0, i, 4, j + LEAD)
                    if j % 2:
                        out = latent_high(i * 2 + c0 + j // 2)
                        act.activation(out, zw[:, j // 2], ACT.Copy).then_inc(lat_hi, 1)

            def root(k, dst):
                act.wait_ge(inv_ready, k)
                act.activation(dst[:, SEQ:], rtmp[:], ACT.Sqrt).then_inc(rfac_ready, 1)

            for j in range(4):
                split_at(N_LAT + j + LEAD)
                if j == 1:
                    root(2, rfac)
                if j % 2:
                    act.activation(latent_high(j // 2), zw[:, j // 2], ACT.Copy).then_inc(lat_hi, 1)
            with act.Fori(1, KQ // 2) as i:
                latent_pair(N_LAT, i, 0)
            square_last(zt[:, (KQ - 1) % 2])
            nkv = N_LAT + 2 * KQ
            for j in range(2 * KKV):
                split_at(nkv + j + LEAD)
                if j == 2:
                    root(3, rq)
                if j % 2:
                    act.activation(latent_high(KQ + j // 2), zw[:, (j // 2) % 2], ACT.Copy).then_inc(lat_hi, 1)
            square_last(zt[:, (KQ + KKV - 1) % 2])

            def swap_halves(k):
                act.wait_ge(rope_z, k)
                if k > 1:
                    act.wait_ge(rotated, k - 1)
                for q in range(4):
                    src = zt[32 * (q ^ 1):32 * (q ^ 1) + 32, (k - 1) % 2]
                    c = act.activation(zs[32 * q:32 * q + 32], src, ACT.Copy)
                c.then_inc(rope_s, 1)

            for j in range(2):
                split_at(nkv + 2 * KKV + j + LEAD)
                if j == 1:
                    root(4, rkv)
                    swap_halves(1)
            for j in range(N_VM - N_PE):
                split_at(N_PE + j + LEAD)
                for m in range(pe_tiles_ending(j)[0], pe_tiles_ending(j)[1]):
                    swap_halves(2 + m)
            for j in range(N_MLA - N_VM):
                split_at(N_VM + j + LEAD)

            def mla_pair(i, first):
                for b in range(2):
                    for j in range(4):
                        if isinstance(i, int):
                            split_at(N_MLA + i * 8 + b * 4 + j + LEAD)
                        else:
                            split_in(N_MLA, i, 8, b * 4 + j + LEAD)
                        if not (first and b == 0):
                            slot_ops(j, i * 2 + (b + A_MLA - 1), i * 2 + (b - 1), "mla", i * 2 + (b + G_MLA - 1))

            mla_pair(0, True)
            with act.Fori(1, MH // 2) as i:
                mla_pair(i, False)
            for j in range(4):
                split_at(N_WOO + j + LEAD)
                slot_ops(j, A_MLA + MH - 1, MH - 1, "mla", G_MLA + MH - 1)
            with act.Fori(1, KD // 2 - 1) as i:
                for j in range(4):
                    split_in(N_WOO, i, 4, j + LEAD)
            for j in range(4):
                split_at(N_END - 4 + j + LEAD)
            act.wait_ge(x_new, 2 * KD)
            square_last(zt[:, (KD - 1) % 2])
            root(5, rfac)
            act.wait_ge(spread_ready, 6)
            act.activation(rfac[:, 0:SEQ], PT[:, 0, 0:SEQ], ACT.Copy).then_inc(factor_copied, 1)
            for k, c in enumerate(POOL_OUT):
                act.wait_ge(y_ready_p, k + 1)
                act.dma_start(y_out[:, 2 * c:2 * c + 2, :], yw[:, 2 * c:2 * c + 2, :]).then_inc(stored_p, 16)
            act.wait_ge(stored_p, 16 * len(POOL_OUT))

        @block.vector
        def _(dve):
            chain = Tally(dve, dve_chain)
            link = chain.link

            marks = {}

            def mark(s):
                col = marks.setdefault(s.name, len(marks))
                dve.memset(tick[:, col:col + 1], 0.0).then_inc(s, 1)

            def split(n, s):
                dve.wait_ge(hi_split, n + 1)
                dve.tensor_tensor(wL[:, s], raw[:, s], wH[:, s].bitcast(f32), SUB).then_inc(lo_split, 1)

            def split_at(n):
                if n < N_END:
                    split(n, n % R)

            def split_in(n0, i, per, j):
                split(i * per + (n0 + j), (n0 + j) % R)

            def take_tile(out, t, factor):
                dve.tensor_tensor(out, proj[:, t % 2, 0:SEQ], factor, MUL).then_inc(tile_taken, 1)

            RF = rfac[:, 0:SEQ]

            def take_gate(t):
                take_tile(gate_z[:], t, RF)
                mark(gz_ready)

            def add_max(out, a, b, top):
                return dve.tensor_tensor_reduce(out=out, in0=a, in1=b, scale=1.0, scalar=-3.0e38,
                                                op0=ADD, op1=MAX, accum_out=top)

            def logits(a, kind, h=None):
                dve.wait_ge(scores_ready, a + 1)
                probs = PROBS[kind][0]
                if kind != "mla":
                    first = 16 * DG
                    want = (a + 1) * first if kind == "dil" else a * 16 + 16 * (DH * DG - DH + 1)
                    dve.wait_ge(bias_loaded, want)
                dve.memset(tick[:, 15:16], 0.0)
                if kind == "dil":
                    for g in range(DG):
                        add_max(probs[:, g, 0:P], S[:, g, 0:P], bias[:, g, P:SEQ], mx[:, 0, g:g + 1])
                        top = add_max(probs[:, g, P:TW], S[:, g, P:TW], bias[:, g, :], mx[:, 1, g:g + 1])
                    link(top)
                    link(dve.tensor_reduce(mx1[:], mx[:], AX.X, MAX))
                    dve.tensor_scalar(nmx[:, :, 0], mx1[:], -SC_EVEN, None, MUL).then_inc(logits_ready, 1)
                if kind == "nsa":
                    for g in range(2):
                        add_max(probs[:, g, 0:P], S[:, g, 0:P], bias[:, 0, P:SEQ], mx[:, 0, g + 1:g + 2])
                        add_max(probs[:, g, P:TW], S[:, g, P:TW], bias[:, 0, :], mx[:, 1, g + 1:g + 2])
                    cb = cbias[:, h] if isinstance(h, int) else cbias[:, ds(h, 1), :].rearrange("p a n -> p (a n)")
                    link(dve.tensor_tensor(pcmp[:].rearrange("p t n -> p (t n)"), S[:, 2, 0:NT * NCMP], cb, ADD))
                    link(dve.tensor_reduce(mx[:, :, 0], pcmp[:], AX.X, MAX))
                    dve.tensor_scalar(nmx[:], mx[:], -SC_EVEN, None, MUL)
                    for t in range(NT):
                        c = dve.tensor_scalar(pcmp[:, t], pcmp[:, t], mx[:, t, 0:1], None, SUB)
                    c.then_inc(logits_ready, 1)
                if kind == "mla":
                    add_max(probs[:, 0, 0:P], S[:, 0, 0:P], cmask_m[:, 0:P], mx[:, 0, 0:1])
                    link(add_max(probs[:, 0, P:TW], S[:, 0, P:TW], cmask_m[:, P:TW], mx[:, 1, 0:1]))
                    dve.tensor_scalar(nmx[:, :, 0], mx[:, :, 0], -SC_MLA, None, MUL).then_inc(logits_ready, 1)

            def scale_probs(a, kind, h=None):
                dve.wait_ge(exp_ready, a + 1)
                probs = PROBS[kind][0]
                if kind == "dil":
                    link(dve.reciprocal(coef[:, :, 0], den[:, :, 0]))
                    dve.tensor_scalar(probs[:, :, 0:P], probs[:, :, 0:P], coef[:, 0, 0:1], None, MUL)
                    dve.tensor_scalar(probs[:, :, P:TW], probs[:, :, P:TW], coef[:, 1, 0:1], None,
                                      MUL).then_inc(probs_ready, 1)
                if kind == "nsa":
                    link(dve.tensor_reduce(den[:, :, 0], pcmp[:], AX.X, ADD))
                    link(dve.reciprocal(coef[:], den[:]))
                    gs = g3s[:, h] if isinstance(h, int) else g3s[:, ds(h, 1)].rearrange("p a t g -> p (a t) g")
                    link(dve.tensor_tensor(coef[:], coef[:], gs, MUL))
                    for t in range(NT):
                        dve.scalar_tensor_tensor(pcmp_s[:, t], pcmp[:, t], coef[:, t, 0:1], cvalid[:, t], MUL, MUL)
                    for g in range(2):
                        dve.tensor_scalar(probs[:, g, 0:P], probs[:, g, 0:P], coef[:, 0, g + 1:g + 2], None, MUL)
                        c = dve.tensor_scalar(probs[:, g, P:TW], probs[:, g, P:TW],
                                              coef[:, 1, g + 1:g + 2], None, MUL)
                    c.then_inc(probs_ready, 1)
                if kind == "mla":
                    link(dve.reciprocal(coef[:, :, 0], den[:, :, 0]))
                    dve.tensor_scalar(probs[:, 0, 0:P], probs[:, 0, 0:P], coef[:, 0, 0:1], None, MUL)
                    dve.tensor_scalar(probs[:, 0, P:TW], probs[:, 0, P:TW], coef[:, 1, 0:1], None,
                                      MUL).then_inc(probs_ready, 1)

            def gate_silu(a):
                dve.wait_ge(gt_ready, a + 1)
                link(dve.scalar_tensor_tensor(gate_g[:], gate_t[:], 1.0, gate_z[:], ADD, MUL))

            def mix(a):
                dve.wait_ge(out_ready, a + 1)
                dve.scalar_tensor_tensor(mixf[:], O[:, 0, 0:SEQ], 0.5, gate_g[:], MUL, MUL).then_inc(out_taken, 1)

            def mix_low(a, idx):
                dve.wait_ge(mix_hi, a + 1)
                if isinstance(idx, int):
                    hi, lo = mixH[:, idx], mixL[:, idx]
                else:
                    hi = mixH[:, ds(idx, 1), :].rearrange("p a n -> p (a n)")
                    lo = mixL[:, ds(idx, 1), :].rearrange("p a n -> p (a n)")
                dve.tensor_tensor(lo, mixf[:], hi.bitcast(f32), SUB).then_inc(mix_lo, 1)

            def slot_ops(j, a, idx, kind, h=None):
                if j == 0:
                    logits(a, kind, h)
                if j == 1:
                    scale_probs(a, kind, h)
                    gate_silu(a)
                if kind == "dil":
                    if j == 6:
                        mix(a)
                    if j == 7:
                        mix_low(a, idx)
                elif j == 3:
                    mix(a)
                    if kind == "mla":
                        mix_low(a, idx)

            def take_norm(use, k, n):
                dve.wait_ge(ms_ready, ms_count(use))
                if k > 1:
                    dve.wait_ge(rfac_ready, k - 1)
                link(dve.tensor_scalar(rvar[:], MS[:, 0, SEQ:SEQ + NT], 1.0 / n, EPS, MUL, ADD))
                mark(ms_taken)
                dve.reciprocal(rtmp[:], rvar[:]).then_inc(inv_ready, 1)

            def refine(dst, k):
                dve.wait_ge(rfac_ready, k)
                r = dst[:, SEQ:]
                link(dve.tensor_tensor(rnew[:], r, r, MUL))
                link(dve.scalar_tensor_tensor(rnew[:], rnew[:], -0.5, rvar[:], MUL, MUL))
                link(dve.scalar_tensor_tensor(r, rnew[:], 1.5, r, ADD, MUL))
                for t in range(NT):
                    c = dve.tensor_scalar(diag[:, t], ident[:], r[:, t:t + 1], None, MUL)
                c.then_inc(diag_ready, 1)

            def spread(dst, k):
                dve.wait_ge(spread_ready, k)
                link(dve.tensor_copy(dst[:, 0:SEQ], O[:, 0, 0:SEQ]))

            for c in range(KD):
                dve.wait_ge(h_hi, c + 1)
                dve.scalar_tensor_tensor(hL[:, c], xT[:, c], nrm[:, 0, c:c + 1], hH[:, c].bitcast(f32),
                                         MUL, SUB).then_inc(h_lo, 1)
                if c % 2 and c // 2 < R:
                    split_at(c // 2)
            dve.wait_ge(g3_hi, 1)
            dve.tensor_tensor(g3L[:], g3w[:], g3H[:].bitcast(f32), SUB).then_inc(g3_lo, 1)
            dve.wait_ge(ms_ready, U_BIAS + 1)
            link(dve.scalar_tensor_tensor(rows[:], MS[0:HEADS_B, 0, 0:RRW], ROOT, rmask[:], MUL, ADD))
            mark(ms_taken)
            mark(rows_ready)

            def take_values(c):
                for t in range(NT):
                    out = (vt[:, t, c * 512:(c + 1) * 512] if isinstance(c, int) else vt[:, t, ds(c * 512, 512)])
                    src = (banks[:, 2 * c + t] if isinstance(c, int) else
                           banks[:, ds(c * 2 + t, 1)].rearrange("p a n -> p (a n)"))
                    dve.tensor_scalar(out, src, rfac[:, SEQ + t:SEQ + t + 1], None,
                                      MUL).then_inc(tile_taken, 1)

            for j in range(PB):
                if j < 4:
                    dve.wait_ge(squares, j + 1)
                    dve.tensor_reduce(sq4[:, j], sq0[:, j % 2].rearrange("p c n -> p n c"), AX.X,
                                      ADD).then_inc(squares_used, 1)
                if j + LEAD >= R:
                    split_at(j + LEAD)
                if j == 3:
                    dve.wait_ge(ms_ready, U_CBIAS + 1)
                    psum = MS[:, 0, 0:64].rearrange("p (t h) -> p h t", h=NSA_HEADS)
                    msk = cmask[:].rearrange("p (a t) -> p a t", a=1).to_broadcast([P, NSA_HEADS, NT * NCMP])
                    dve.scalar_tensor_tensor(cbias[:], psum, ROOT, msk, MUL, ADD).then_inc(ms_taken, 1)
                if j == 5:
                    take_norm(U_NORM0, 1, D_MODEL)
                if j == 6:
                    refine(rfac, 1)
                    dve.wait_ge(ms_ready, U_GATE3 + 1)
                    link(dve.tensor_copy(g3c, MS[0:24, 0, 0:SEQ]))
                    mark(ms_taken)
                    mark(g3c_ready)
                if j == 7:
                    spread(rfac, 1)
            dve.wait_ge(piece_used, PB)
            take_values(0)
            dve.wait_ge(ms_ready, U_GATE3T + 1)
            for t in range(NT):
                c = dve.tensor_scalar(g3z[:, t], MS[:, 0, 24 * t:24 * t + 24],
                                      rfac[:, SEQ + t:SEQ + t + 1], None, MUL)
            link(c)
            mark(ms_taken)
            mark(g3z_ready)
            with dve.Fori(1, 4) as i:
                for j in range(PB):
                    split_in(N_V, i, PB, j + LEAD)
                dve.wait_ge(piece_used, i * PB + PB)
                take_values(i)

            def dilated(d, attend):
                for j in range(16):
                    if attend:
                        slot_ops(j, d - 1, d + (NSA_HEADS - 1), "dil")
                        split_in(N_DIL, d, 16, j + LEAD)
                    else:
                        split_at(N_DIL + j + LEAD)
                    if not attend and j == 2:
                        dve.wait_ge(g3t_ready, 1)
                        for t in range(NT):
                            dve.tensor_scalar(g3s[:, :, t, :], g3t[:, t].rearrange("p (h b) -> p h b", b=3),
                                              1.0, 0.5, ADD, MUL)
                    if j % 2:
                        t = j // 2
                        dve.wait_ge(piece_used, d * 16 + (N_DIL + j + 1))
                        if t < 3:
                            take_tile(qd[:, t], t, RF)
                        elif t < 6:
                            take_tile(kd[:, t - 3], t, RF)
                        elif t == 6:
                            out = kvc[:, d] if isinstance(d, int) else kvc[:, ds(d, 1), :].rearrange("p a n -> p (a n)")
                            take_tile(out, t, RF)
                        else:
                            take_gate(t)

            dilated(0, False)
            with dve.Fori(1, DH) as d:
                chain.turn(d - 1, DVE_TURN["dil"])
                dilated(d, True)
            chain.leave(DH - 1)
            j = 0
            for p, kind in enumerate(KSW_ORDER):
                if p == len(KSW_ORDER) - 1:
                    dve.wait_ge(piece_used, N_NSA)
                    link(dve.tensor_copy(csum, MS[0:16, 0].rearrange("p (w a e) -> p w a e", w=2, a=2)))
                    mark(ms_taken)
                    mark(csum_ready)
                if p == 0:
                    dve.wait_ge(tile_taken, T_KSW)
                    for w in range(2):
                        for g in range(NSA_GROUPS):
                            src = kvc[:, 2 * w + g].rearrange("p (n s) -> p s n", s=NSA_BLOCK)
                            pos = posT[:, w].rearrange("p (s a) -> p s a", a=1).to_broadcast([P, NSA_BLOCK, NCMP])
                            c = dve.tensor_tensor(kcp[:, w, :, g * NCMP:(g + 1) * NCMP], src, pos, ADD)
                    c.then_inc(kcp_ready, 1)
                if kind == "k":
                    slot_ops(j, DH - 1, NSA_HEADS + DH - 1, "dil")
                if p == 0:
                    dve.wait_ge(kc_hi, 1)
                    dve.tensor_tensor(kcHL[:, :, :, 8:16], kcp[:], kcHL[:, :, :, 0:8].bitcast(f32),
                                      SUB).then_inc(kc_lo, 1)
                split_at(N_KSW + p + LEAD)
                if kind == "k":
                    if j % 2:
                        dve.wait_ge(piece_used, N_KSW + p + 1)
                        take_tile(ksw[:, j // 2], j // 2, RF)
                    j += 1
            dve.wait_ge(ms_ready, ms_count(U_CMPS))
            link(dve.tensor_copy(cz[:].rearrange("p w n -> p (w n)"), MS[:, 0, 0:16]))
            mark(ms_taken)
            mark(cz_ready)
            dve.wait_ge(ct_ready, 1)
            link(dve.scalar_tensor_tensor(cs[:], ct[:], 1.0, cz[:], ADD, MUL))
            dve.tensor_scalar(cs[:], cs[:], 0.5, None, MUL).then_inc(cs_ready, 1)

            def nsa(h, attend):
                for j in range(4):
                    if not attend and j == 3:
                        dve.wait_ge(ms_ready, ms_count(U_CMP2))
                        dve.tensor_copy(kcmp[:], MS[:, 0, 0:8])
                        for g in range(NSA_GROUPS):
                            c = dve.tensor_copy(vcmp[:, g], MS[0:NCMP, 0, P * (g + 1):P * (g + 2)])
                        c.then_inc(ms_taken, 1)
                    if attend:
                        if j < 3:
                            slot_ops(j, h + (A_NSA - 1), h - 1, "nsa", h - 1)
                        split_in(N_NSA, h, 4, j + LEAD)
                        if j == 3:
                            slot_ops(j, h + (A_NSA - 1), h - 1, "nsa", h - 1)
                    else:
                        split_at(N_NSA + j + LEAD)
                    if j % 2:
                        dve.wait_ge(piece_used, h * 4 + (N_NSA + j + 1))
                        if j == 1:
                            take_tile(qa[:], 0, RF)
                        else:
                            take_gate(1)
                            if attend:
                                mix_low(h + (A_NSA - 1), h - 1)

            nsa(0, False)
            with dve.Fori(1, NSA_HEADS) as h:
                chain.turn(h - 1, DVE_TURN["nsa"])
                nsa(h, True)
            chain.leave(NSA_HEADS - 1)

            tile = 0
            for j in range(KD * EVEN_MIX // PB):
                if j < 3:
                    slot_ops(j, A_MLA - 1, NSA_HEADS - 1, "nsa", NSA_HEADS - 1)
                if j != 4:
                    split_at(N_WOE + j + LEAD)
                if j == 3:
                    slot_ops(j, A_MLA - 1, NSA_HEADS - 1, "nsa", NSA_HEADS - 1)
                    mix_low(A_MLA - 1, NSA_HEADS - 1)
                ending = []
                while tile < KD and woe_end(tile) < (j + 1) * PB:
                    mid = woe_mid(tile)
                    if mid is None:
                        dve.wait_ge(piece_used, N_WOE + j + 1)
                    else:
                        dve.wait_ge(mid_tile, mid + 1)
                    src = S[:, 1, 0:SEQ] if tile == 2 else proj[:, (T_WOE + tile) % 2, 0:SEQ]
                    xc = xr[:, tile % XR]
                    dve.wait_ge(xr_loaded[tile % XR], 16 * (tile // XR + 1))
                    link(dve.tensor_tensor(xc, xc, src, ADD))
                    mark(tile_taken)
                    mark(x_new)
                    ending.append(tile)
                    tile += 1
                if j == 4:
                    split_at(N_WOE + j + LEAD)
                for k in ending:
                    dve.wait_ge(h_hi, KD + k + 1)
                    dve.scalar_tensor_tensor(hL[:, k], xr[:, k % XR], nrm[:, 1, k:k + 1],
                                             hH[:, k].bitcast(f32), MUL, SUB).then_inc(h_lo, 1)

            def latent(c, t, par, weight):
                if not isinstance(c, int) or 2 <= c <= KQ:
                    dve.wait_ge(squares, c + 3)
                elif c == KQ + 1:
                    dve.wait_ge(last_square, 2)
                elif c > KQ + 1:
                    dve.wait_ge(squares, c + 2)
                link(dve.tensor_tensor(zt[:, par], proj[:, t % 2, 0:SEQ], RF, MUL))
                link(dve.tensor_scalar(zw[:, par], zt[:, par], weight, None, MUL))
                mark(tile_taken)
                mark(lat_z)
                dve.wait_ge(lat_hi, c + 1)
                if isinstance(c, int):
                    hi, lo = latH[:, c], latL[:, c]
                else:
                    hi = latH[:, ds(c, 1), :].rearrange("p a n -> p (a n)")
                    lo = latL[:, ds(c, 1), :].rearrange("p a n -> p (a n)")
                dve.tensor_tensor(lo, zw[:, par], hi.bitcast(f32), SUB).then_inc(lat_lo, 1)

            for j in range(4):
                split_at(N_LAT + j + LEAD)
                if j == 1:
                    take_norm(U_NORM1, 2, D_MODEL)
                    refine(rfac, 2)
                    spread(rfac, 2)
                if j % 2:
                    dve.wait_ge(piece_used, N_LAT + j + 1)
                    latent(j // 2, T_LAT + j // 2, j // 2, qn[:, j // 2:j // 2 + 1])
            with dve.Fori(1, KQ // 2) as i:
                chain.turn(i - 1, DVE_TURN["lat"])
                for j in range(4):
                    split_in(N_LAT, i, 4, j + LEAD)
                    if j % 2:
                        dve.wait_ge(piece_used, i * 4 + (N_LAT + j + 1))
                        c = i * 2 + j // 2
                        latent(c, T_LAT + j // 2, j // 2, qn[:, ds(c, 1)])
            chain.leave(KQ // 2 - 1)
            nkv, tkv = N_LAT + 2 * KQ, T_LAT + KQ
            for j in range(2 * KKV):
                split_at(nkv + j + LEAD)
                if j == 2:
                    take_norm(U_NORMQ, 3, QR)
                if j == 3:
                    refine(rq, 3)
                if j == 6:
                    spread(rq, 3)
                if j % 2:
                    c = j // 2
                    dve.wait_ge(piece_used, nkv + j + 1)
                    latent(KQ + c, tkv + c, c % 2, kvn[:, c:c + 1])

            def take_rotary(t, factor, k):
                if k == 1:
                    dve.wait_ge(squares, 2 + KQ + KKV)
                if k == 2:
                    dve.wait_ge(last_square, 3)
                if k > 2:
                    dve.wait_ge(rotated, k - 2)
                link(dve.tensor_tensor(zt[:, (k - 1) % 2], proj[:, t % 2, 0:SEQ], factor, MUL))
                mark(tile_taken)
                mark(rope_z)

            for j in range(2):
                split_at(nkv + 2 * KKV + j + LEAD)
            dve.wait_ge(piece_used, nkv + 2 * KKV + 2)
            take_rotary(T_LAT + KQ + KKV, RF, 1)
            take_norm(U_NORMKV, 4, KVR)
            for j in range(N_VM - N_PE):
                split_at(N_PE + j + LEAD)
                for m in range(pe_tiles_ending(j)[0], pe_tiles_ending(j)[1]):
                    if m % 2 == 0:
                        dve.wait_ge(mid_tile, MID_PE + m // 2 + 1)
                    else:
                        dve.wait_ge(piece_used, N_PE + j + 1)
                    take_rotary(T_PE + m, rq[:, 0:SEQ], 2 + m)
                if j == 0:
                    refine(rkv, 4)
                if j == 3:
                    spread(rkv, 4)
            for j in range(8):
                split_at(N_VM + j + LEAD)
                if j % 2:
                    dve.wait_ge(piece_used, N_VM + j + 1)
                    for t in range(NT):
                        dve.tensor_scalar(vt[:, t, 512 * (j // 2):512 * (j // 2) + 512],
                                          banks[:, VM_BANKS[j // 2] + t], rkv[:, SEQ + t:SEQ + t + 1], None,
                                          MUL).then_inc(tile_taken, 1)

            def mla_pair(i, first):
                for b in range(2):
                    for j in range(4):
                        jj = b * 4 + j
                        if not (first and b == 0):
                            slot_ops(j, i * 2 + (b + A_MLA - 1), i * 2 + (b - 1), "mla")
                        if isinstance(i, int):
                            split_at(N_MLA + i * 8 + jj + LEAD)
                        else:
                            split_in(N_MLA, i, 8, jj + LEAD)
                        t = T_MLA + 3 * b
                        if j == 1:
                            dve.wait_ge(mid_tile, i * 2 + (b + MID_MLA + 1))
                            take_tile(qm[:], t, rq[:, 0:SEQ])
                            dve.wait_ge(piece_used, i * 8 + (N_MLA + jj + 1))
                            take_tile(km[:], t + 1, rkv[:, 0:SEQ])
                        if j == 3:
                            dve.wait_ge(piece_used, i * 8 + (N_MLA + jj + 1))
                            take_gate(t + 2)

            dve.wait_ge(consts_odd, 32)
            mla_pair(0, True)
            with dve.Fori(1, MH // 2) as i:
                chain.turn(i - 1, DVE_TURN["mla"])
                mla_pair(i, False)
            chain.leave(MH // 2 - 1)

            dve.wait_ge(rotated, 1 + MH // 2)

            def last_residual(c, s, par, t):
                if not isinstance(c, int) or c >= 2:
                    dve.wait_ge(squares, c + (1 + KQ + KKV))
                if isinstance(c, int):
                    yc, nw = yw[:, c], nrm[:, 2, c:c + 1]
                else:
                    yc, nw = yw[:, ds(c, 1), :].rearrange("p a n -> p (a n)"), nrm[:, 2, ds(c, 1)]
                link(dve.tensor_tensor(zt[:, par], xr[:, s], proj[:, t % 2, 0:SEQ], ADD))
                mark(tile_taken)
                mark(x_new)
                link(dve.tensor_scalar(yc, zt[:, par], nw, None, MUL))

            for j in range(4):
                slot_ops(j, A_MLA + MH - 1, MH - 1, "mla")
                split_at(N_WOO + j + LEAD)
            dve.wait_ge(mid_tile, MID_WOO + 1)
            dve.wait_ge(xm_loaded[0], 16)
            last_residual(0, 0, 0, T_WOO)
            dve.wait_ge(piece_used, N_WOO + 4)
            dve.wait_ge(xm_loaded[1], 16)
            last_residual(1, 1, 1, T_WOO + 1)

            for j in range(4):
                split_at(N_WOO + 4 + j + LEAD)
                if j % 2:
                    c = 2 + j // 2
                    dve.wait_ge(piece_used, N_WOO + 4 + j + 1)
                    dve.wait_ge(xm_loaded[c], 16)
                    last_residual(c, c, c % 2, T_WOO + c)
            with dve.Fori(1, KD // XR - 1) as i:
                chain.turn(i - 1, DVE_TURN["woo"])
                for j in range(8):
                    split_in(N_WOO, i, 8, j + LEAD)
                    if j % 2:
                        c = j // 2
                        dve.wait_ge(piece_used, i * 8 + (N_WOO + j + 1))
                        dve.wait_ge(xm_loaded[c], i * 16 + 16)
                        last_residual(i * 4 + c, c, c % 2, T_WOO + c)
            chain.leave(KD // XR - 2)
            for j in range(8):
                split_at(N_END - 8 + j + LEAD)
                if j % 2:
                    c = KD - 4 + j // 2
                    dve.wait_ge(piece_used, N_END - 8 + j + 1)
                    dve.wait_ge(xm_loaded[c % XR], 16 * (c // XR + 1))
                    last_residual(c, c % XR, c % 2, T_WOO + c)
            take_norm(U_NORMF, 5, D_MODEL)
            refine(rfac, 5)
            dve.wait_ge(spread_ready, 5)
            for c in DVE_OUT:
                scale_out(dve, c, O[:, 0, 0:SEQ]).then_inc(y_ready, 1)

        @block.tensor
        def _(pe):
            def piece(b, n, s):
                if b % PB == 0:
                    pe.wait_ge(lo_split, n + 1)
                cols = slice((b % PB) * P, (b % PB + 1) * P)
                return wH[:, s, cols], wL[:, s, cols]

            def products(out, WH, WL, aH, aL, start, stop):
                pe.matmul(out, WH, aH, start=start, stop=False)
                pe.matmul(out, WH, aL, start=False, stop=False)
                return pe.matmul(out, WL, aH, start=False, stop=stop)

            def done(last, b, mid=False):
                if b % PB == PB - 1:
                    last.then_inc(piece_used, 1)
                elif mid:
                    last.then_inc(mid_tile, 1)

            def tile_part(out, b0, n0, i, per, aH, aL, order, first=True, final=True, ready=None):
                for k, src in enumerate(order):
                    b = b0 + k
                    n = n0 + b // PB
                    if ready is not None:
                        ready(src)
                    WH, WL = piece(b, i * per + n, n % R)
                    stop = final and k == len(order) - 1
                    last = products(out, WH, WL, aH[:, src], aL[:, src], first and k == 0, stop)
                    done(last, b, stop)

            def tile_free(t):
                pe.wait_ge(tile_taken, t - 1)

            def full(t, par, b0, n0, i, per, aH, aL, count, ready=None):
                tile_free(t)
                tile_part(proj[:, par % 2, 0:SEQ], b0, n0, i, per, aH, aL, range(count), ready=ready)

            def values(t, b0, n0, i, per, aH, aL, count, outs, halfway=None):
                if t is not None:
                    tile_free(t + 1)
                for k in range(count):
                    b = b0 + 4 * k
                    n = n0 + b // PB
                    if halfway is not None and k == count // 2:
                        halfway()
                    if b % PB == 0:
                        pe.wait_ge(lo_split, i * per + (n + 1))
                    s, half = n % R, slice((b % PB) * P, (b % PB + 4) * P)
                    for tt in range(NT):
                        toks = slice(tt * P, (tt + 1) * P)
                        out = outs[tt]
                        pe.matmul(out, aH[:, k, toks], wH[:, s, half], start=k == 0, stop=False)
                        pe.matmul(out, aL[:, k, toks], wH[:, s, half], start=False, stop=False)
                        last = pe.matmul(out, aH[:, k, toks], wL[:, s, half], start=False, stop=k == count - 1)
                    if b % PB == 4:
                        last.then_inc(piece_used, 1)

            def norm_sums(use, k):
                pe.wait_ge(acc_ready, k)
                pe.wait_ge(ms_taken, use)
                pe.wait_ge(last_square, k)
                for t in range(NT):
                    tk = slice(t * P, (t + 1) * P)
                    pe.matmul(MS[:, 0, SEQ + t:SEQ + t + 1], nrm_sum[:, tk], ones[:, 0:1], start=True, stop=False)
                    last = pe.matmul(MS[:, 0, SEQ + t:SEQ + t + 1], zs[:, tk], ones[:, 0:1], start=False, stop=True)
                last.then_inc(ms_ready, 1)

            def spread(k, out=O):
                pe.wait_ge(diag_ready, k)
                pe.matmul(out[:, 0, 0:SEQ], ones[:], diag[:].rearrange("p t n -> p (t n)"),
                          start=True, stop=True).then_inc(spread_ready, 1)

            def start_up(j):
                if j == 1:
                    pe.wait_ge(consts_bias, 16 * 5)
                    pe.matmul(MS[0:HEADS_B, 0, 0:RRW], tab[:], oneh[:], start=True, stop=True).then_inc(ms_ready, 1)
                if j == 3:
                    pe.wait_ge(ms_taken, U_CBIAS)
                    for tn in range(NT * NCMP):
                        last = pe.matmul(MS[:, 0, tn * 8:tn * 8 + 8], oneh_c[:, tn], tab[:, 0:NSA_HEADS],
                                         start=True, stop=True)
                    last.then_inc(ms_ready, 1)
                if j == 4:
                    pe.wait_ge(ms_taken, U_NORM0)
                    pe.wait_ge(squares_used, 4)
                    for t in range(NT):
                        for k in range(4):
                            last = pe.matmul(MS[:, 0, SEQ + t:SEQ + t + 1], sq4[:, k, t * P:(t + 1) * P],
                                             ones[:, 0:1], start=k == 0, stop=k == 3)
                    last.then_inc(ms_ready, 1)
                if j == 6:
                    spread(1)
                if j == 5:
                    pe.wait_ge(ms_taken, U_GATE3)
                    pe.wait_ge(g3_lo, 1)
                    for k in range(KD):
                        last = products(MS[0:24, 0, 0:SEQ], g3H[:, k], g3L[:, k], hH[:, k], hL[:, k],
                                        k == 0, k == KD - 1)
                    last.then_inc(ms_ready, 1)
                if j == 7:
                    pe.wait_ge(g3c_ready, 1)
                    pe.wait_ge(ms_taken, U_GATE3T)
                    for t in range(NT):
                        last = pe.transpose(MS[:, 0, 24 * t:24 * t + 24], g3c[:, t * P:(t + 1) * P], ident[0:24, 0:24])
                    last.then_inc(ms_ready, 1)

            def score(g, q, k, more=None):
                for t, (lo, hi) in enumerate(((0, P), (P, TW))):
                    last = pe.matmul(S[:, g, lo:hi], q(t), k(hi - lo), start=True, stop=more is None)
                    if more is not None:
                        last = pe.matmul(S[:, g, lo:hi], more[0](t), more[1](hi - lo), start=False, stop=True)
                return last

            def toks(x):
                return (lambda t: x[:, t * P:(t + 1) * P]), (lambda n: x[:, 0:n])

            def scores(kind, taken, gg=0, rot=None):
                pe.wait_ge(tile_taken, taken - 1)
                if kind == "dil":
                    for g in range(DG):
                        last = score(g, toks(qd[:, g])[0], toks(kd[:, g])[1])
                if kind == "nsa":
                    for g in range(2):
                        last = score(g, toks(qa[:])[0], toks(ksw[:, 2 * gg + g])[1])
                    for t in range(NT):
                        last = pe.matmul(S[:, 2, NCMP * t:NCMP * (t + 1)], qa[:, t * P:(t + 1) * P],
                                         kcmp[:, NCMP * gg:NCMP * (gg + 1)], start=True, stop=True)
                if kind == "mla":
                    base = slice(64 * rot, 64 * rot + 64)
                    last = score(0, toks(qm[:])[0], toks(km[:])[1],
                                 (toks(qpc[base])[0], toks(kpe[base])[1]))
                last.then_inc(scores_ready, 1)

            def transposes(kind, k, g, a=None, out=PT):
                if a is not None:
                    pe.wait_ge(probs_ready, a + 1)
                if out is PT and (not isinstance(k, int) or k > 0):
                    pe.wait_ge(pt_taken, k)
                for c in range(3):
                    cols = slice(c * P, (c + 1) * P)
                    last = pe.transpose(out[:, 0, cols], PROBS[kind][0][:, g, cols], ident[:])
                last.then_inc(pt_ready, 1)

            def cmp_transposes(k):
                for t in range(NT):
                    last = pe.transpose(S[0:NCMP, 2, P * (t + 1):P * (t + 2)], pcmp_s[:, t], ident[:])
                last.then_inc(pt_ready, 1)

            def weigh(kind, k, v0, v1, g, first, final):
                pe.wait_ge(pt_taken, k + 1)
                probsT = PROBS[kind][1]
                pe.matmul(O[:, 0, 0:SEQ], v0, probsT[:, g, 0:SEQ], start=first, stop=False)
                return pe.matmul(O[:, 0, P:SEQ], v1, probsT[:, g, SEQ:TW], start=False, stop=final)

            def slot_ops(j, a, kind, taken, g0, gg=0, rot=None):
                if j == 0:
                    if kind == "mla":
                        pe.wait_ge(qp_copied, rot[1])
                    scores(kind, taken, gg, None if rot is None else rot[0])
                if kind == "dil":
                    if j == 4:
                        if not isinstance(a, int) or a > 0:
                            pe.wait_ge(out_taken, a)
                        pe.wait_ge(v_copied, a + 1)
                    if 4 <= j <= 6:
                        g = j - 4
                        last = weigh(kind, g0 + g, v_cur[:, g, 0], v_cur[:, g, 1], g, g == 0, g == DG - 1)
                        if g == DG - 1:
                            last.then_inc(out_ready, 1)
                    if 3 <= j <= 5:
                        transposes(kind, g0 + j - 3, j - 3, a if j == 3 else None)
                if kind == "nsa":
                    if j == 2:
                        transposes(kind, g0, 0, a)
                        cmp_transposes(g0 + 1)
                        transposes(kind, g0 + 2, 1, out=S)
                    if j == 3:
                        pe.wait_ge(out_taken, a)
                        weigh(kind, g0, vt[:, 0, gg * P:(gg + 1) * P], vt[:, 1, gg * P:(gg + 1) * P], 0, True, False)
                        pe.wait_ge(pt_taken, g0 + 2)
                        pe.matmul(O[:, 0, 0:SEQ], vcmp[:, gg], pcmpT[:], start=False, stop=False)
                        weigh(kind, g0 + 2, vt[:, 0, 256 + gg * P:256 + (gg + 1) * P],
                              vt[:, 1, 256 + gg * P:256 + (gg + 1) * P], 1, False, True).then_inc(out_ready, 1)
                if kind == "mla":
                    if j == 2:
                        transposes(kind, g0, 0, a)
                    if j == 3:
                        pe.wait_ge(out_taken, a)
                        pe.wait_ge(v_copied, a - (A_MLA - DH - 1))
                        weigh(kind, g0, v_head[:, 0], v_head[:, 1], 0, True, True).then_inc(out_ready, 1)

            pe.wait_ge(pool_set, 1)
            for _ in range(WARM):
                pe.matmul(MS[:, 0, 0:P], ones[:], ones[:], start=True, stop=True)

            def h_ready(k):
                pe.wait_ge(h_lo, k + 1)

            def first_values():
                for k in range(KD):
                    h_ready(k)
                    b, n, s = 4 * k, k // 2, (k // 2) % R
                    if b % PB == 0:
                        pe.wait_ge(lo_split, n + 1)
                    half = slice((b % PB) * P, (b % PB + 4) * P)
                    for tt in range(NT):
                        tk = slice(tt * P, (tt + 1) * P)
                        out = proj[:, tt, :]
                        pe.matmul(out, hH[:, k, tk], wH[:, s, half], start=k == 0, stop=False)
                        pe.matmul(out, hL[:, k, tk], wH[:, s, half], start=False, stop=False)
                        last = pe.matmul(out, hH[:, k, tk], wL[:, s, half], start=False, stop=k == KD - 1)
                    if b % PB == 4:
                        last.then_inc(piece_used, 1)
                        start_up(k // 2)

            first_values()
            with pe.Fori(1, 4) as i:
                values(None, 0, N_V, i, PB, hH, hL, KD,
                       outs=[banks[:, ds(i * 2 + t, 1)].rearrange("p a n -> p (a n)") for t in range(NT)],
                       halfway=lambda: pe.wait_ge(ms_taken, U_CMP))

            def dilated(d, attend):
                for t in range(8):
                    for half in range(2):
                        j = 2 * t + half
                        if attend:
                            slot_ops(j, d - 1, "dil", d * 8 + T_DIL, (d - 1) * DG)
                        if half == 0 and (attend or t >= 2):
                            tile_free(d * 8 + (T_DIL + t))
                        if j == 0 and not attend:
                            pe.wait_ge(tile_taken, NT)
                        tile_part(proj[:, t % 2, 0:SEQ], 16 * t + 8 * half, N_DIL, d, 16, hH, hL,
                                  range(8 * half, 8 * half + 8), half == 0, half == 1)

            dilated(0, False)
            with pe.Fori(1, DH) as d:
                dilated(d, True)

            j = m = 0
            for p, kind in enumerate(KSW_ORDER):
                n = N_KSW + p
                if kind == "k":
                    slot_ops(j, DH - 1, "dil", T_KSW, (DH - 1) * DG)
                    t, half = j // 2, j % 2
                    if half == 0:
                        tile_free(T_KSW + t)
                    tile_part(proj[:, t % 2, 0:SEQ], PB * p, N_KSW, 0, 0, hH, hL,
                              range(8 * half, 8 * half + 8), half == 0, half == 1)
                    j += 1
                    continue
                if m == 0:
                    pe.wait_ge(kc_lo, 1)
                    pe.wait_ge(ms_taken, U_CMP)
                pe.wait_ge(lo_split, n + 1)
                for b in range(PB):
                    w, s = m // 8, (m % 8) * PB + b
                    last = pe.matmul(MS[0:16, 0, 256 * w:256 * w + 256], kcHL[:, w, s],
                                     w_hl[:, :, n % R, b * P:(b + 1) * P], start=s == 0, stop=s == NSA_BLOCK - 1)
                last.then_inc(piece_used, 1)
                m += 1

            def nsa(h, gg, attend):
                for t in range(2):
                    for half in range(2):
                        j = 2 * t + half
                        at = {2: 4, 3: 3}.get(j, 0)
                        if half == 0:
                            if j == 0 and attend:
                                slot_ops(0, h + (A_NSA - 1), "nsa", h * 2 + T_NSA, (h - 1) * 3 + G_NSA, gg)
                            tile_free(h * 2 + (T_NSA + t))
                        for lo, hi in ((0, at), (at, 8)):
                            if lo == at and attend and j >= 2:
                                slot_ops(j, h + (A_NSA - 1), "nsa", h * 2 + T_NSA, (h - 1) * 3 + G_NSA, gg)
                            if lo < hi:
                                tile_part(proj[:, t % 2, 0:SEQ], 8 * j + lo, N_NSA, h, 4, hH, hL,
                                          range(8 * half + lo, 8 * half + hi), half == 0 and lo == 0,
                                          half == 1 and hi == 8)
                        if not attend and j == 0:
                            pe.wait_ge(csum_ready, 1)
                            pe.wait_ge(ms_taken, U_CMPS)
                            for w in range(2):
                                for part in range(2):
                                    last = pe.matmul(MS[:, 0, 8 * w:8 * w + 8], csum[:, w, part], sel[:],
                                                     start=part == 0, stop=part == 1)
                            last.then_inc(ms_ready, 1)
                        if not attend and j == 2:
                            pe.wait_ge(cs_ready, 1)
                            pe.wait_ge(ms_taken, U_CMP2)
                            pe.matmul(MS[:, 0, 0:8], w2[:, 0], cs[:, 0], start=True, stop=True)
                            for g in range(NSA_GROUPS):
                                last = pe.matmul(MS[0:NCMP, 0, P * (g + 1):P * (g + 2)],
                                                 cs[:, 1, NCMP * g:NCMP * (g + 1)], w2[:, 1], start=True, stop=True)
                            last.then_inc(ms_ready, 1)

            nsa(0, 0, False)
            pe.wait_ge(ms_taken, U_CMP2 + 1)
            for gg, (lo, hi) in enumerate(((1, NSA_HPG + 1), (NSA_HPG + 1, NSA_HEADS))):
                with pe.Fori(lo, hi) as h:
                    nsa(h, gg, True)

            def woe_outs(tile):
                return S[:, 1, 0:SEQ] if tile == 2 else proj[:, (T_WOE + tile) % 2, 0:SEQ]

            early = list(range(NSA_HEADS, EVEN_MIX)) + list(range(NSA_HEADS - 1))
            attn_at = {0: 0, 20: 2, 27: 3}
            b = 0
            for tile in range(3):
                for k, src in enumerate(early):
                    if b in attn_at:
                        slot_ops(attn_at[b], A_MLA - 1, "nsa", T_WOE, G_MLA - 3, NSA_GROUPS - 1)
                    if k == 0 and tile < 2:
                        tile_free(T_WOE + tile)
                    if b == 0:
                        pe.wait_ge(mix_lo, A_MLA - 1)
                    tile_part(woe_outs(tile), b, N_WOE, 0, 0, mixH, mixL, [src], k == 0, False)
                    b += 1
            pe.wait_ge(mix_lo, A_MLA)
            for tile in range(3):
                tile_part(woe_outs(tile), b, N_WOE, 0, 0, mixH, mixL, [NSA_HEADS - 1], False, True)
                b += 1
            for tile in range(3, KD):
                tile_free(T_WOE + tile)
                tile_part(woe_outs(tile), b, N_WOE, 0, 0, mixH, mixL, early + [NSA_HEADS - 1])
                b += EVEN_MIX

            def h2_ready(k):
                pe.wait_ge(h_lo, KD + k + 1)

            full(T_LAT, T_LAT, 0, N_LAT, 0, 0, hH, hL, KD, ready=h2_ready)
            norm_sums(U_NORM1, 1)
            tile_free(T_LAT + 1)
            for lo in (0, 8):
                tile_part(proj[:, (T_LAT + 1) % 2, 0:SEQ], KD + lo, N_LAT, 0, 0, hH, hL, range(lo, lo + 8),
                          lo == 0, lo == 8)
                if lo == 0:
                    spread(2)
            with pe.Fori(1, KQ // 2) as i:
                for t in range(2):
                    full(i * 2 + (T_LAT + t), T_LAT + t, KD * t, N_LAT, i, 4, hH, hL, KD)
            for c in range(KKV + 1):
                full(T_LAT + KQ + c, T_LAT + KQ + c, KD * (KQ + c), N_LAT, 0, 0, hH, hL, KD)
                if c == 0:
                    norm_sums(U_NORMQ, 2)
                if c == 2:
                    spread(3)
            norm_sums(U_NORMKV, 3)

            b = 0
            for m in range(MH // 2):
                if m == 0:
                    pe.wait_ge(lat_lo, KQ)
                full(T_PE + m, T_PE + m, b, N_PE, 0, 0, latH, latL, KQ)
                b += KQ
                if m == 1:
                    spread(4)
            pe.wait_ge(lat_lo, KQ + KKV)
            kvH, kvL = latH[:, KQ:], latL[:, KQ:]
            for c in range(4):
                if c == 1:
                    pe.wait_ge(tile_taken, T_VM)
                if c == 3:
                    pe.wait_ge(tile_taken, T_VM + NT)
                values(None, 16 * c, N_VM, 0, 0, kvH, kvL, KKV, outs=[banks[:, VM_BANKS[c] + t] for t in range(NT)])

            def mla_pair(i, first):
                for bb in range(2):
                    t0 = T_MLA + 3 * bb
                    attend = not (first and bb == 0)
                    at = 32 * bb

                    def ops(j):
                        if attend:
                            slot_ops(j, i * 2 + (bb + A_MLA - 1), "mla", i * 6 + t0, i * 2 + (bb + G_MLA - 1),
                                     rot=(1 - bb, i + bb))

                    ops(0)
                    if first and bb == 0:
                        pe.wait_ge(tile_taken, T_VM + 2 * NT)
                    else:
                        tile_free(i * 6 + t0)
                    tile_part(proj[:, t0 % 2, 0:SEQ], at, N_MLA, i, 8, latH, latL, range(KQ))
                    if attend:
                        tile_free(i * 6 + (t0 + 1))
                    tile_part(proj[:, (t0 + 1) % 2, 0:SEQ], at + KQ, N_MLA, i, 8, kvH, kvL, range(KKV))
                    ops(2)
                    tile_free(i * 6 + (t0 + 2))
                    tile_part(proj[:, (t0 + 2) % 2, 0:SEQ], at + 16, N_MLA, i, 8, hH, hL, range(8), True, False)
                    ops(3)
                    tile_part(proj[:, (t0 + 2) % 2, 0:SEQ], at + 24, N_MLA, i, 8, hH, hL, range(8, 16), False, True)

            mla_pair(0, True)
            with pe.Fori(1, MH // 2) as i:
                mla_pair(i, False)

            attn_at = {0: 0, 16: 2, 24: 3}
            b = 0
            for tile in range(2):
                for k in range(KD - 1):
                    if b in attn_at:
                        slot_ops(attn_at[b], A_MLA + MH - 1, "mla", T_WOO, G_MLA + MH - 1, rot=(1, MH // 2))
                    if k == 0:
                        tile_free(T_WOO + tile)
                    if b == 0:
                        pe.wait_ge(mix_lo, A_MLA + MH - 1)
                    tile_part(proj[:, (T_WOO + tile) % 2, 0:SEQ], b, N_WOO, 0, 0, mixH, mixL, [k], k == 0, False)
                    b += 1
            pe.wait_ge(mix_lo, A_MLA + MH)
            for tile in range(2):
                tile_part(proj[:, (T_WOO + tile) % 2, 0:SEQ], b, N_WOO, 0, 0, mixH, mixL, [KD - 1], False, True)
                b += 1
            with pe.Fori(1, KD // 2) as i:
                for t in range(2):
                    full(i * 2 + (T_WOO + t), T_WOO + t, KD * t, N_WOO, i, 4, mixH, mixL, KD)
            norm_sums(U_NORMF, 4)
            spread(5)
            spread(5, PT)


def woe_end(tile):
    return 33 + tile if tile < 3 else EVEN_MIX * (tile + 1) - 1


def woe_mid(tile):
    return None if woe_end(tile) % PB == PB - 1 else [t for t in range(KD) if woe_end(t) % PB != PB - 1].index(tile)


def pe_tiles_ending(j):
    ends = [m for m in range(MH // 2) if (KQ * (m + 1) - 1) // PB == j]
    return (ends[0], ends[-1] + 1) if ends else (0, 0)


def _bucket(d):
    exact = BUCKETS // 2
    d = np.maximum(d, 0)
    big = exact + (np.log(np.maximum(d, 1).astype(np.float32) / exact) / math.log(MAX_DIST / exact)
                   * (BUCKETS - exact)).astype(np.int32)
    return np.where(d < exact, d, np.minimum(big, BUCKETS - 1))


def _constants():
    f = np.float32
    d = SEQ - 1 - np.arange(RRW)
    onehot = ((_bucket(d)[None, :] == np.arange(BUCKETS)[:, None]) & (d >= 0)[None, :]).astype(f)
    row_mask = np.zeros((HEADS_B, RRW), f)
    row_mask[:, d < 0] = NEG
    for g, (window, step) in enumerate(DIL):
        out = (d > window) | (d % step != 0) | (d < 0)
        row_mask[NSA_HEADS + g * DH:NSA_HEADS + (g + 1) * DH, out] = NEG
    t = np.arange(SEQ).reshape(NT, P)
    dist = t[:, None, :] - (np.arange(NCMP) * NSA_BLOCK + NSA_BLOCK - 1)[None, :, None]
    onehot_cmp = ((_bucket(dist)[None] == np.arange(BUCKETS)[:, None, None, None]) & (dist >= 0)[None])
    onehot_cmp = onehot_cmp.astype(f).reshape(BUCKETS, NT * NCMP, P)
    valid = (dist >= 0).transpose(2, 0, 1)
    cmp_mask = np.where(valid, 0.0, NEG).astype(f).reshape(P, NT * NCMP)
    tri = np.where(np.arange(P)[None, :] <= np.arange(P)[:, None], 0.0, NEG).astype(f)
    causal = np.concatenate([tri, np.zeros((P, P), f), tri], 1)
    half = ROPE // 2
    freqs = (1.0 / (f(10000.0) ** (np.arange(half, dtype=f) / f(half)))).astype(f)
    ang = freqs[:, None] * np.arange(SEQ, dtype=f)[None, :]
    cos, sin = np.cos(ang).astype(f), np.sin(ang).astype(f)
    cs = np.stack([np.tile(cos, (4, 1)), np.concatenate([-sin, sin, -sin, sin], 0)], 1)
    return dict(onehot=onehot, onehot_cmp=onehot_cmp, row_mask=row_mask, cmp_mask=cmp_mask,
                cmp_valid=valid.astype(f), causal=causal, rope_cs=cs, ident_in=np.eye(P, dtype=f),
                sel_in=np.tile(np.eye(8, dtype=f), (2, 1)))


def _stream(ev, evo, od, qb, kvb, odo, w1):
    blocks = []

    def put(w, k, col):
        blocks.append(w[k * P:(k + 1) * P, col:col + P] if isinstance(col, int) else w[k * P:(k + 1) * P, col])

    q_a, kv_a, gate_a, qkv_b = 0, 1024, 2584, 3608
    gate_b = qkv_b + 3 * DG * DH * HD
    kc, vc, ks, vs, kw, vw = (kv_a + 256 * n for n in range(6))
    vb = qkv_b + 2 * DG * DH * HD
    chunks = [[vs, vs + P, vw, vw + P]] + [[vb + (g * DH + d) * P for d in range(DH)] for g in range(DG)]
    for cols in chunks:
        for k in range(KD):
            for c in cols:
                put(ev, k, c)
    for d in range(DH):
        cols = [qkv_b + (g * DH + d) * P for g in range(DG)]
        cols += [qkv_b + (DG * DH + g * DH + d) * P for g in range(DG)]
        cols += [(kc, kc + P, vc, vc + P)[d], gate_b + d * P]
        for c in cols:
            for k in range(KD):
                put(ev, k, c)
    keys = [(k, c) for c in (ks, kw, ks + P, kw + P) for k in range(KD)]
    cmp1 = [(w, s) for w in range(2) for s in range(NSA_BLOCK)]
    for kind in KSW_ORDER:
        for _ in range(PB):
            if kind == "k":
                put(ev, *keys.pop(0))
            else:
                w, s = cmp1.pop(0)
                put(w1[w], s, 0)
    for h in range(NSA_HEADS):
        for c in (q_a + h * P, gate_a + h * P):
            for k in range(KD):
                put(ev, k, c)
    early = list(range(NSA_HEADS, EVEN_MIX)) + list(range(NSA_HEADS - 1))
    for tile in range(3):
        for k in early:
            put(evo, k, tile * P)
    for tile in range(3):
        put(evo, NSA_HEADS - 1, tile * P)
    for tile in range(3, KD):
        for k in early + [NSA_HEADS - 1]:
            put(evo, k, tile * P)
    for c in range(KQ + KKV):
        for k in range(KD):
            put(od, k, c * P)
    twice = np.tile(np.arange(QR + KVR, QR + KVR + ROPE), 2)
    for k in range(KD):
        put(od, k, twice)
    hq, hkv = NOPE + ROPE, NOPE + MV
    for m in range(MH // 2):
        cols = np.concatenate([np.arange(ROPE) + (2 * m + b) * hq + NOPE for b in range(2)])
        for k in range(KQ):
            put(qb, k, cols)
    for c in range(4):
        for k in range(KKV):
            for h in range(4 * c, 4 * c + 4):
                put(kvb, k, h * hkv + NOPE)
    for h in range(MH):
        for k in range(KQ):
            put(qb, k, h * hq)
        for k in range(KKV):
            put(kvb, k, h * hkv)
        for k in range(KD):
            put(od, k, QR + KVR + ROPE + h * P)
    for tile in range(2):
        for k in range(KD - 1):
            put(odo, k, tile * P)
    for tile in range(2):
        put(odo, KD - 1, tile * P)
    for tile in range(2, KD):
        for k in range(KD):
            put(odo, k, tile * P)
    assert len(blocks) == N_END * PB
    out = np.empty((N_END, P, PB, P), np.float32)
    for n, b in enumerate(blocks):
        out[n // PB, :, n % PB] = b
    return out.reshape(N_END, P, PW)


def kernel(x, rel_bias, norm_w, final_norm_w, ev_w_in, nsa_cmp_pos, nsa_cmp_w1, nsa_cmp_w2,
           ev_w_out, od_w_in, mla_q_norm, mla_w_qb, mla_kv_norm, mla_w_kvb, od_w_out):
    import concourse.bacc as bacc
    from concourse.bass_utils import run_bass_kernel_spmd

    a = {k: np.asarray(v) for k, v in dict(
        x=x, ev=ev_w_in, evo=ev_w_out, od=od_w_in, qb=mla_w_qb, kvb=mla_w_kvb, odo=od_w_out,
        w1=nsa_cmp_w1, w2=nsa_cmp_w2, pos=nsa_cmp_pos, tab=rel_bias, nw=norm_w, fw=final_norm_w,
        qn=mla_q_norm, kvn=mla_kv_norm).items()}
    arrays = dict(
        x_in=a["x"][0].T.reshape(KD, P, SEQ).transpose(1, 0, 2),
        w_stream=_stream(a["ev"][0], a["evo"][0], a["od"][0], a["qb"][0], a["kvb"][0], a["odo"][0], a["w1"][0]),
        w_gate3=a["ev"][0][:, 2560:2584].reshape(KD, P, 24).transpose(1, 0, 2),
        w_cmp2=a["w2"][0].transpose(1, 0, 2),
        cmp_pos=a["pos"][0].transpose(2, 0, 1),
        table=a["tab"],
        norms=np.concatenate([a["nw"], a["fw"][None]], 0).reshape(3, KD, P).transpose(2, 0, 1),
        q_norm=a["qn"][0].reshape(KQ, P).T,
        kv_norm=a["kvn"][0].reshape(KKV, P).T,
        **_constants())
    nc = bacc.Bacc("TRN2", target_bir_lowering=False, num_devices=1)
    args, feeds = {}, {}
    for name, v in arrays.items():
        v = np.ascontiguousarray(v)
        feeds[name + "_dram"] = v
        args[name] = nc.dram_tensor(name + "_dram", v.shape, mybir.dt.from_np(v.dtype), kind="ExternalInput").ap()
    y = nc.dram_tensor("y_dram", (P, KD, SEQ), mybir.dt.float32, kind="ExternalOutput").ap()
    trunk(nc, y_out=y, **args)
    r = run_bass_kernel_spmd(nc, [feeds], core_ids=[0])
    got = r.results[0]["y_dram"]
    return got.transpose(2, 1, 0).reshape(1, SEQ, D_MODEL)
```
